# Optimizing a Trainium2 kernel written in Bass

```python
import math
import jax, jax.numpy as jnp
from jax import lax
import numpy as np

D_MODEL = 2048
BATCH = 1
SEQ = 512
DEPTH = 2

GRID_W = 64
CTX_LEN = 256
D_MIX = D_MODEL
D_CONV = D_MIX // 4
D_ATTN = D_MIX // 2
D_POOL = D_MIX // 4
N_HEADS = 8
V_DIM = D_ATTN // N_HEADS
QK_DIM = V_DIM // 2
ATTN_SCALE = QK_DIM ** -0.5
Q_BLOCK = 128
CONV_W = 3
POOL_WINDOWS = (2, 4, 8, 16)
N_POOL_GROUPS = 4
POOL_GROUP = D_POOL // N_POOL_GROUPS
ROPE_THETA = 10000.0
LN_EPS = 1e-5
RMS_EPS = 1e-5
DEEPNORM_ALPHA = (2 * DEPTH) ** 0.25
DEEPNORM_BETA = (8 * DEPTH) ** -0.25
SPLIT_SIZES = (D_CONV, D_CONV, D_CONV, D_CONV, D_ATTN, D_ATTN, D_ATTN, D_ATTN, D_POOL, D_POOL)
SPLIT_POINTS = tuple(int(s) for s in np.cumsum(SPLIT_SIZES)[:-1])
D_IN = sum(SPLIT_SIZES)
ATT_K_OFF = 4 * D_CONV + D_ATTN
ATT_V_END = 4 * D_CONV + 3 * D_ATTN


def _layernorm(x, g, b):
    xf = x.astype(jnp.float32)
    mu = jnp.mean(xf, axis=-1, keepdims=True)
    var = jnp.mean(jnp.square(xf - mu), axis=-1, keepdims=True)
    return ((xf - mu) * lax.rsqrt(var + LN_EPS) * g + b).astype(x.dtype)

def _qk_heads(t):
    return t.reshape(t.shape[0], t.shape[1], N_HEADS, 2, QK_DIM)

def _v_heads(t):
    return t.reshape(t.shape[0], t.shape[1], N_HEADS, V_DIM)

def _rope_axial(x, rows, cols):
    half = QK_DIM // 2
    n = half // 2
    inv = ROPE_THETA ** (-jnp.arange(n, dtype=jnp.float32) / n)

    def rot(v, pos):
        ang = pos.astype(jnp.float32)[:, None] * inv
        cos = jnp.cos(ang)[None, :, None, None, :]
        sin = jnp.sin(ang)[None, :, None, None, :]
        v1, v2 = v[..., :n], v[..., n:]
        return jnp.concatenate([v1 * cos - v2 * sin, v1 * sin + v2 * cos], axis=-1)

    xf = x.astype(jnp.float32)
    return jnp.concatenate([rot(xf[..., :half], rows), rot(xf[..., half:], cols)], axis=-1).astype(x.dtype)

def _diff_attn(qb, k_all, v_all, lam):
    s = jnp.einsum('bqhid,bkhid->bhiqk', qb.astype(jnp.float32) * ATTN_SCALE, k_all.astype(jnp.float32))
    p = jax.nn.softmax(s, axis=-1)
    a = p[:, :, 0] - lam * p[:, :, 1]
    return jnp.einsum('bhqk,bkhe->bqhe', a.astype(v_all.dtype), v_all)

def _diff_subln(o, g, lam_init):
    of = o.astype(jnp.float32)
    y = of * lax.rsqrt(jnp.mean(jnp.square(of), axis=-1, keepdims=True) + RMS_EPS) * g * (1.0 - lam_init)
    return y.reshape(o.shape[0], o.shape[1], D_ATTN).astype(o.dtype)

def _short_conv(u, b_gate, c_gate, g, w):
    v = c_gate * u
    T = u.shape[1]
    vp = jnp.pad(v, ((0, 0), (1, 1), (0, 0)))
    y = vp[:, :T] * w[0] + vp[:, 1:T + 1] * w[1] + vp[:, 2:] * w[2]
    return jax.nn.silu(g) * (b_gate * y)

def _multiscale_pool(u, g, pool_w_l, pool_scale_l):
    B, T, _ = u.shape
    ug = u.reshape(B, T, N_POOL_GROUPS, POOL_GROUP).astype(jnp.float32)
    csum = jnp.concatenate([jnp.zeros_like(ug[:, :1]), jnp.cumsum(ug, axis=1)], axis=1)
    t = jnp.arange(T)
    diffs = []
    for gi, w in enumerate(POOL_WINDOWS):
        lo = jnp.clip(t - w // 2, 0, T)
        hi = jnp.clip(t + w - w // 2, 0, T)
        mean = (csum[:, hi, gi] - csum[:, lo, gi]) / (hi - lo).astype(jnp.float32)[None, :, None]
        diffs.append(mean - ug[:, :, gi])
    d = jnp.stack(diffs, axis=2).astype(u.dtype)
    y = jnp.einsum('btgc,gcd->btgd', d, pool_w_l).reshape(B, T, D_POOL) * pool_scale_l
    return jax.nn.silu(g) * y

def _mix_output(parts, att, lam_init, conv_w_l, subln_g_l, pool_w_l, pool_scale_l, w_out_l):
    cu, cb, cc, cg, _q, _k, _v, ag, pu, pg = parts
    y_conv = _short_conv(cu, cb, cc, cg, conv_w_l)
    y_attn = jax.nn.silu(ag) * _diff_subln(att, subln_g_l, lam_init)
    y_pool = _multiscale_pool(pu, pg, pool_w_l, pool_scale_l)
    return jnp.concatenate([y_conv, y_attn, y_pool], axis=-1) @ w_out_l

def first_inputs(seed: int = 0) -> dict:
    key = jax.random.key(seed)
    ks = jax.random.split(key, 18)
    f32 = jnp.float32

    def nrm(k, shape, s):
        return s * jax.random.normal(k, shape, f32)

    return {
        'x': nrm(ks[0], (BATCH, SEQ, D_MODEL), 1.0),
        'c': nrm(ks[1], (BATCH, D_MODEL), 1.0),
        'ctx': nrm(ks[2], (BATCH, CTX_LEN, D_MODEL), 1.0),
        'c_ctx': nrm(ks[3], (D_MODEL,), 1.0),
        'w_mod': nrm(ks[4], (DEPTH, D_MODEL, 3 * D_MODEL), 0.5 * D_MODEL ** -0.5),
        'b_mod': nrm(ks[5], (DEPTH, 3 * D_MODEL), 0.02),
        'w_in': nrm(ks[6], (DEPTH, D_MODEL, D_IN), D_MODEL ** -0.5),
        'conv_w': nrm(ks[7], (DEPTH, CONV_W, D_CONV), CONV_W ** -0.5),
        'lam_q1': nrm(ks[8], (DEPTH, QK_DIM), 0.1),
        'lam_k1': nrm(ks[9], (DEPTH, QK_DIM), 0.1),
        'lam_q2': nrm(ks[10], (DEPTH, QK_DIM), 0.1),
        'lam_k2': nrm(ks[11], (DEPTH, QK_DIM), 0.1),
        'subln_g': 1.0 + nrm(ks[12], (DEPTH, V_DIM), 0.02),
        'pool_w': nrm(ks[13], (DEPTH, N_POOL_GROUPS, POOL_GROUP, POOL_GROUP), POOL_GROUP ** -0.5),
        'pool_scale': 1.0 + nrm(ks[14], (DEPTH, D_POOL), 0.02),
        'w_out': nrm(ks[15], (DEPTH, D_MIX, D_MODEL), DEEPNORM_BETA * D_MIX ** -0.5),
        'ln_g': 1.0 + nrm(ks[16], (DEPTH, D_MODEL), 0.02),
        'ln_b': nrm(ks[17], (DEPTH, D_MODEL), 0.02),
    }

def first_block(x, c, ctx, c_ctx, w_mod, b_mod, w_in, conv_w, lam_q1, lam_k1, lam_q2, lam_k2,
              subln_g, pool_w, pool_scale, w_out, ln_g, ln_b):
    B, L, _ = x.shape
    ROWS = L // GRID_W
    rows = jnp.repeat(jnp.arange(ROWS, dtype=jnp.int32), GRID_W)
    cols = jnp.broadcast_to(jnp.arange(GRID_W, dtype=jnp.int32)[None, :], (ROWS, GRID_W)).reshape(-1)
    n_blk = L // Q_BLOCK
    xl, xc = x, ctx
    for l in range(DEPTH):
        last = l == DEPTH - 1
        sh_l, sc_l, g_l = jnp.split(jax.nn.silu(c) @ w_mod[l] + b_mod[l], 3, axis=-1)
        sh_c, sc_c, g_c = jnp.split(jax.nn.silu(c_ctx) @ w_mod[l] + b_mod[l], 3, axis=-1)
        hl = xl * (1.0 + sc_l[:, None, :]) + sh_l[:, None, :]
        hc = xc * (1.0 + sc_c) + sh_c
        lam_init = 0.8 - 0.6 * math.exp(-0.3 * l)
        lam = (jnp.exp(jnp.sum(lam_q1[l].astype(jnp.float32) * lam_k1[l].astype(jnp.float32)))
               - jnp.exp(jnp.sum(lam_q2[l].astype(jnp.float32) * lam_k2[l].astype(jnp.float32)))
               + lam_init)
        parts_l = jnp.split(hl @ w_in[l], SPLIT_POINTS, axis=-1)
        ql = _rope_axial(_qk_heads(parts_l[4]), rows, cols)
        kl = _rope_axial(_qk_heads(parts_l[5]), rows, cols)
        vl = _v_heads(parts_l[6])
        if last:
            kc, vc = jnp.split(hc @ w_in[l][:, ATT_K_OFF:ATT_V_END], 2, axis=-1)
            parts_c = None
        else:
            parts_c = jnp.split(hc @ w_in[l], SPLIT_POINTS, axis=-1)
            kc, vc = parts_c[5], parts_c[6]
        kc = _qk_heads(kc)
        vc = _v_heads(vc)
        k_all = jnp.concatenate([kc, kl], axis=1)
        v_all = jnp.concatenate([vc, vl], axis=1)
        q_blocks = ql.reshape(B, n_blk, Q_BLOCK, N_HEADS, 2, QK_DIM).swapaxes(0, 1)
        att_l = lax.map(lambda qb: _diff_attn(qb, k_all, v_all, lam), q_blocks)
        att_l = att_l.swapaxes(0, 1).reshape(B, L, N_HEADS, V_DIM)
        out_l = _mix_output(parts_l, att_l, lam_init, conv_w[l], subln_g[l], pool_w[l], pool_scale[l], w_out[l])
        xl_new = _layernorm(DEEPNORM_ALPHA * xl + g_l[:, None, :] * out_l, ln_g[l], ln_b[l])
        if not last:
            att_c = _diff_attn(_qk_heads(parts_c[4]), kc, vc, lam)
            out_c = _mix_output(parts_c, att_c, lam_init, conv_w[l], subln_g[l], pool_w[l], pool_scale[l], w_out[l])
            xc = _layernorm(DEEPNORM_ALPHA * xc + g_c * out_c, ln_g[l], ln_b[l])
        xl = xl_new
    return xl


DEPTH_2 = 1

D_MIX_2 = D_MODEL
HEAD_DIM = 64
D_ATTN_2 = D_MIX_2 // 2
D_CONV_2 = D_MIX_2 - D_ATTN_2
N_Q_HEADS = D_ATTN_2 // HEAD_DIM
N_KV_HEADS = 4
GQA_GROUP = N_Q_HEADS // N_KV_HEADS
D_KV = N_KV_HEADS * HEAD_DIM
WINDOW = 128
BLOCK = 128
CONV_WIDTH = 31
CONV_GROUPS = D_CONV_2 // HEAD_DIM
N_BUCKETS = 32
MAX_DISTANCE = 128
ALPHA = (2.0 * DEPTH_2) ** 0.25
BETA = (8.0 * DEPTH_2) ** -0.25

SPLIT_SIZES_2 = (D_ATTN_2, D_KV, D_KV, D_ATTN_2, D_CONV_2, D_CONV_2, D_CONV_2)
D_IN_2 = sum(SPLIT_SIZES_2)
SPLIT_POINTS_2 = [int(s) for s in np.cumsum(SPLIT_SIZES_2)[:-1]]


def layer_norm(x, g, b):
    xf = x.astype(jnp.float32)
    mu = jnp.mean(xf, axis=-1, keepdims=True)
    var = jnp.mean(jnp.square(xf - mu), axis=-1, keepdims=True)
    y = (xf - mu) * lax.rsqrt(var + LN_EPS)
    return (y * g.astype(jnp.float32) + b.astype(jnp.float32)).astype(x.dtype)

def t5_bucket(dist):
    max_exact = N_BUCKETS // 2
    d = jnp.maximum(dist, 1).astype(jnp.float32)
    large = max_exact + (jnp.log(d / max_exact) / math.log(MAX_DISTANCE / max_exact)
                         * (N_BUCKETS - max_exact)).astype(jnp.int32)
    large = jnp.minimum(large, N_BUCKETS - 1)
    return jnp.where(dist < max_exact, dist, large)

def banded_sink_attention(q, k, v, rel_bias, sinks):
    B, S = q.shape[0], q.shape[1]
    nb = S // BLOCK
    f32 = jnp.float32
    qb = q.astype(f32).reshape(B, nb, BLOCK, N_KV_HEADS, GQA_GROUP, HEAD_DIM)
    kb = k.astype(f32).reshape(B, nb, BLOCK, N_KV_HEADS, HEAD_DIM)
    vb = v.astype(f32).reshape(B, nb, BLOCK, N_KV_HEADS, HEAD_DIM)
    prev = lambda t: jnp.concatenate([jnp.zeros_like(t[:, :1]), t[:, :-1]], axis=1)
    kw = jnp.concatenate([prev(kb), kb], axis=2)
    vw = jnp.concatenate([prev(vb), vb], axis=2)
    scores = jnp.einsum('bnqhgd,bnkhd->bnhgqk', qb, kw) * (HEAD_DIM ** -0.5)

    qi = jnp.arange(BLOCK, dtype=jnp.int32)[:, None]
    kj = jnp.arange(2 * BLOCK, dtype=jnp.int32)[None, :]
    dist = qi + BLOCK - kj
    in_window = (dist >= 0) & (dist < WINDOW)
    bias = rel_bias.astype(f32)[t5_bucket(jnp.maximum(dist, 0))]
    bias = bias.transpose(2, 0, 1).reshape(N_KV_HEADS, GQA_GROUP, BLOCK, 2 * BLOCK)
    key_pos = jnp.arange(nb, dtype=jnp.int32)[:, None] * BLOCK - BLOCK + kj
    valid = in_window[None] & (key_pos[:, None, :] >= 0)

    scores = jnp.where(valid[None, :, None, None], scores + bias, jnp.finfo(f32).min)
    sink = jnp.broadcast_to(sinks.astype(f32).reshape(1, 1, N_KV_HEADS, GQA_GROUP, 1, 1),
                            scores.shape[:-1] + (1,))
    probs = jax.nn.softmax(jnp.concatenate([scores, sink], axis=-1), axis=-1)[..., :-1]
    out = jnp.einsum('bnhgqk,bnkhd->bnqhgd', probs, vw)
    return out.reshape(B, S, N_Q_HEADS * HEAD_DIM).astype(q.dtype)

def conformer_conv(glu_a, glu_b, conv_w, conv_b, ln_g, ln_b, w_pw, b_pw):
    u = glu_a * jax.nn.sigmoid(glu_b)
    u = lax.conv_general_dilated(
        u, conv_w.reshape(CONV_WIDTH, 1, D_CONV_2).astype(u.dtype),
        window_strides=(1,), padding=[(CONV_WIDTH - 1, 0)],
        dimension_numbers=('NWC', 'WIO', 'NWC'), feature_group_count=D_CONV_2) + conv_b
    u = jax.nn.silu(layer_norm(u, ln_g, ln_b))
    return u @ w_pw + b_pw

def second_inputs(seed: int = 0) -> dict:
    key = jax.random.key(seed)
    ks = jax.random.split(key, 20)
    n = jax.random.normal
    f32 = jnp.float32
    x = n(ks[0], (BATCH, SEQ, D_MODEL), f32)
    c = n(ks[1], (BATCH, D_MODEL), f32)
    w_ada = 0.5 * D_MODEL ** -0.5 * n(ks[2], (DEPTH_2, D_MODEL, 3 * D_MODEL), f32)
    b_ada = 0.01 * n(ks[3], (DEPTH_2, 3 * D_MODEL), f32)
    col_scale = jnp.ones((D_IN_2,), f32).at[D_ATTN_2 + D_KV:D_ATTN_2 + 2 * D_KV].set(BETA)
    w_in = D_MODEL ** -0.5 * n(ks[4], (DEPTH_2, D_MODEL, D_IN_2), f32) * col_scale
    rel_bias = 0.5 * n(ks[5], (N_BUCKETS, N_Q_HEADS), f32)
    sinks = n(ks[6], (DEPTH_2, N_Q_HEADS), f32)
    conv_w = CONV_WIDTH ** -0.5 * n(ks[7], (DEPTH_2, CONV_WIDTH, D_CONV_2), f32)
    conv_b = 0.01 * n(ks[8], (DEPTH_2, D_CONV_2), f32)
    conv_ln_g = 1.0 + 0.01 * n(ks[9], (DEPTH_2, D_CONV_2), f32)
    conv_ln_b = 0.01 * n(ks[10], (DEPTH_2, D_CONV_2), f32)
    w_pw = BETA * D_CONV_2 ** -0.5 * n(ks[11], (DEPTH_2, D_CONV_2, D_CONV_2), f32)
    b_pw = 0.01 * n(ks[12], (DEPTH_2, D_CONV_2), f32)
    w_out = BETA * D_MIX_2 ** -0.5 * n(ks[13], (DEPTH_2, D_MIX_2, D_MODEL), f32)
    ln_g = 1.0 + 0.01 * n(ks[14], (DEPTH_2, D_MODEL), f32)
    ln_b = 0.01 * n(ks[15], (DEPTH_2, D_MODEL), f32)
    return {"x": x, "c": c, "w_ada": w_ada, "b_ada": b_ada, "w_in": w_in,
            "rel_bias": rel_bias, "sinks": sinks, "conv_w": conv_w, "conv_b": conv_b,
            "conv_ln_g": conv_ln_g, "conv_ln_b": conv_ln_b, "w_pw": w_pw, "b_pw": b_pw,
            "w_out": w_out, "ln_g": ln_g, "ln_b": ln_b}

def second_block(x, c, w_ada, b_ada, w_in, rel_bias, sinks, conv_w, conv_b, conv_ln_g,
              conv_ln_b, w_pw, b_pw, w_out, ln_g, ln_b):
    c_act = jax.nn.silu(c)
    for l in range(DEPTH_2):
        mod = (c_act @ w_ada[l] + b_ada[l])[:, None, :]
        shift, scale, gate = jnp.split(mod, 3, axis=-1)
        h = x * (1.0 + scale) + shift
        proj = h @ w_in[l]
        q, k, v, g_attn, glu_a, glu_b, g_conv = jnp.split(proj, SPLIT_POINTS_2, axis=-1)
        y_attn = banded_sink_attention(q, k, v, rel_bias, sinks[l]) * jax.nn.silu(g_attn)
        y_conv = conformer_conv(glu_a, glu_b, conv_w[l], conv_b[l], conv_ln_g[l], conv_ln_b[l],
                                w_pw[l], b_pw[l]) * jax.nn.silu(g_conv)
        y = jnp.concatenate([y_attn, y_conv], axis=-1) @ w_out[l]
        x = layer_norm(ALPHA * x + gate * y, ln_g[l], ln_b[l])
    return x


_first_inputs = second_inputs


def second_inputs(seed=0):
    import zlib

    import numpy as np

    out = dict(_first_inputs(seed))
    spreads = {}
    factors = {'b_ada': 8.0,
     'rel_bias': 8.0,
     'sinks': 8.0,
     'conv_b': 8.0,
     'conv_ln_g': 8.0,
     'conv_ln_b': 8.0,
     'b_pw': 8.0,
     'ln_g': 5.574,
     'ln_b': 5.499}
    for name, (base, spread) in spreads.items():
        noise = np.random.default_rng([zlib.crc32(name.encode()), seed]).standard_normal(out[name].shape)
        drawn = base * np.exp(spread * noise) if base else spread * noise
        out[name] = __import__('jax').numpy.asarray(drawn.astype(out[name].dtype))
    for name, factor in factors.items():
        out[name] = (out[name] * factor).astype(out[name].dtype)
    return out


_narrow_inputs = second_inputs


def second_inputs(seed=0):

    out = dict(_narrow_inputs(seed))
    wider = {'rel_bias': 3.31,
     'sinks': 6.63,
     'conv_ln_g': 12.0,
     'conv_ln_b': 12.0,
     'b_pw': 11.45,
     'ln_g': 6.27,
     'ln_b': 6.27}
    for name, times in wider.items():
        mean = out[name].mean()
        out[name] = (mean + times * (out[name] - mean)).astype(out[name].dtype)
    return out


def setup_inputs(seed=0):
    out = dict(first_inputs(seed))
    for name, value in second_inputs(seed + 1).items():
        if name != "x":
            out[name + "_2"] = value
    return out


def reference(
    x, c, ctx, c_ctx, w_mod, b_mod, w_in, conv_w, lam_q1, lam_k1, lam_q2, lam_k2, subln_g,
    pool_w, pool_scale, w_out, ln_g, ln_b, c_2, w_ada_2, b_ada_2, w_in_2, rel_bias_2, sinks_2,
    conv_w_2, conv_b_2, conv_ln_g_2, conv_ln_b_2, w_pw_2, b_pw_2, w_out_2, ln_g_2, ln_b_2,
):
    x = first_block(
        x, c, ctx, c_ctx, w_mod, b_mod, w_in, conv_w, lam_q1, lam_k1, lam_q2, lam_k2, subln_g,
        pool_w, pool_scale, w_out, ln_g, ln_b,
    )
    return second_block(
        x, c_2, w_ada_2, b_ada_2, w_in_2, rel_bias_2, sinks_2, conv_w_2, conv_b_2, conv_ln_g_2,
        conv_ln_b_2, w_pw_2, b_pw_2, w_out_2, ln_g_2, ln_b_2,
    )


_drawn_inputs = setup_inputs


def setup_inputs(seed=0):
    import zlib

    import numpy as np

    out = dict(_drawn_inputs(seed))
    spreads = {}
    factors = {'ctx': 4.619,
     'b_mod': 6.473,
     'lam_q1': 8.0,
     'lam_k1': 8.0,
     'lam_q2': 8.0,
     'lam_k2': 8.0,
     'subln_g': 52.34,
     'pool_scale': 58.128,
     'sinks_2': 21.111,
     'rel_bias_2': 3.016}
    for name, (base, spread) in spreads.items():
        noise = np.random.default_rng([zlib.crc32(name.encode()), seed]).standard_normal(out[name].shape)
        drawn = base * np.exp(spread * noise) if base else spread * noise
        out[name] = __import__('jax').numpy.asarray(drawn.astype(out[name].dtype))
    for name, factor in factors.items():
        out[name] = (out[name] * factor).astype(out[name].dtype)
    return out
```

```python
import math
from contextlib import ExitStack

import numpy as np

import concourse.bass as bass
from concourse import mybir

F32 = mybir.dt.float32
F32R = mybir.dt.float32r
ALU = mybir.AluOpType
ACT = mybir.ActivationFunctionType
AX_X = mybir.AxisListType.X

P = 128
D = 2048
KT = D // P
SEQ, CTX = 512, 256
N_HEADS, QK = 8, 64
N_CONV, N_POOL = 4, 4
WINDOWS = (2, 4, 8, 16)
PAD = max(WINDOWS) // 2
EPS = 1e-5
DEPTH = 2
ALPHA1 = (2.0 * DEPTH) ** 0.25
ALPHA2 = 2.0 ** 0.25
TAPS = 31
BLOCK = 128
NEG = -3.0e38
MC = 256
MOD_TILES = D // P // 4
LAM_INIT = tuple(0.8 - 0.6 * math.exp(-0.3 * l) for l in range(DEPTH))

VECS = [("b_mod0", 48), ("b_mod1", 48), ("b_mod2", 48), ("conv_w0", 12), ("conv_w1", 12),
        ("subln0", 1), ("subln1", 1), ("pool_s0", 4), ("pool_s1", 4),
        ("ln_g0", 16), ("ln_g1", 16), ("ln_g2", 16), ("ln_b0", 16), ("ln_b1", 16), ("ln_b2", 16),
        ("dw", 8 * TAPS), ("dw_b", 8), ("cln_g", 8), ("cln_b", 8), ("b_pw", 8),
        ("c0", 16), ("c1", 16), ("c2", 16)]
VEC_AT = {}
_at = 0
for _n, _w in VECS:
    VEC_AT[_n] = _at
    _at += _w
NVEC = _at

STREAM = [("cconv", 4, 4), ("chead", 8, 4), ("cpool", 4, 2), ("cout", 4, 4),
          ("aconv", 4, 4), ("ahead", 8, 4), ("apool", 4, 2), ("aout", 4, 4),
          ("kv1", 8, 2),
          ("bconv", 4, 4), ("bhead", 8, 4), ("bpool", 4, 2), ("bout", 4, 4),
          ("glu", 8, 2), ("kv2", 1, 4), ("attn2", 8, 2), ("gconv", 4, 2), ("pw", 2, 2), ("out2", 4, 4)]
TILE0 = {}
_at = 0
for _n, _i, _t in STREAM:
    TILE0[_n] = _at
    _at += _i * _t
N_TILES = _at
MODS = [("mod0", 8, 2), ("chead", 8, 1), ("ahead", 8, 2), ("bconv", 4, 2), ("bhead", 8, 2), ("bout", 4, 2)]
CHUNK0 = {}
_at = 0
for _n, _i, _t in MODS:
    CHUNK0[_n] = _at
    _at += _i * _t
MOD_OF = {"mod0": ((0, 1), 0), "chead": ((0, 1), 32), "ahead": ((2, 3), 0), "bconv": ((2,), 32),
          "bhead": ((4,), 0), "bout": ((4,), 32)}
MOD_VEC = (0, 1, 0, 1, 2)
MOD_LAYER = (0, 0, 1, 1, 2)


class At:

    def __init__(self, c, k=0, i=0):
        if isinstance(i, int):
            c, k, i = c + k * i, 0, 0
        self.c, self.k, self.i = c, k, i

    def __add__(self, n):
        return At(self.c + n, self.k, self.i)

    def __sub__(self, n):
        return self + -n

    @property
    def odd(self):
        assert self.k % 2 == 0
        return self.c % 2

    @property
    def half(self):
        assert self.k % 2 == 0
        return At(self.c // 2, self.k // 2, self.i)

    def times(self, n):
        return At(self.c * n, self.k * n, self.i)

    @property
    def val(self):
        return self.i * self.k + self.c if self.k else self.c


def build(nc, A, out):
    with ExitStack() as ctx:
        def sb(name, cols, dt=F32, rows=P):
            return ctx.enter_context(nc.sbuf_tensor(name, [rows, cols], dt))

        def psum(name, cols):
            return ctx.enter_context(nc.psum_tensor(name, [P, cols], F32))

        credits = {}

        def sem(name, credit=0):
            s = ctx.enter_context(nc.semaphore(name))
            credits[id(s)] = credit
            return s

        def dram(name, shape):
            return nc.dram_tensor(name, shape, F32, kind="Internal").ap()

        raw = sb("raw", 2 * D)
        w_hi = sb("w_hi", 2 * D, F32R)
        w_lo = sb("w_lo", 2 * D, F32R)
        h_hi = sb("h_hi", KT * SEQ, F32R)
        h_lo = sb("h_lo", KT * SEQ, F32R)
        xy = sb("xy", KT * SEQ)
        mraw = sb("mraw", 2 * 4 * MC)
        macc = sb("macc", 2 * 2 * MC)
        ev = [sb(f"ev{n}", SEQ) for n in range(4)]
        evt = sb("evt", SEQ)
        work = sb("work", 4608)
        qb = sb("qb", SEQ)
        kb = sb("kb", SEQ + CTX)
        vtok = sb("vtok", 1024)
        rope = sb("rope", 2 * SEQ)
        t1 = sb("t1", SEQ)
        t2 = sb("t2", SEQ)
        vecs = sb("vecs", NVEC)
        modc = sb("modc", 5 * 48)
        csil = sb("csil", 48)
        ident = sb("ident", P)
        ones = sb("ones", P)
        edge = sb("edge", 4 * 16)
        lam = sb("lam", 2 * 8)
        sink = sb("sink", 16)
        small = sb("small", 32)
        assert MOD_TILES == 4

        acc = [psum(f"acc{n}", 512) for n in range(2)]
        S = psum("S", 2048)
        pv = psum("pv", 512)
        misc = psum("misc", 512)
        mod_ps = misc[:, 0:4]

        xy3 = xy[:, :].rearrange("p (k t) -> p k t", t=SEQ)
        maps = [work[:, (SEQ + CTX) * m:(SEQ + CTX) * (m + 1)] for m in range(2)]
        a_t = work[:, 1536:1536 + 6 * SEQ]
        POOLW = 2096
        s2 = [work[:, 1024 * e:1024 * (e + 1)] for e in range(2)]
        k2 = work[:, 2048:3072]

        k_ctx = dram("k_ctx", (DEPTH, N_HEADS, P, CTX))
        v_ctx = dram("v_ctx", (DEPTH, N_HEADS, P, CTX))
        c1_d = dram("c1_d", (P, KT, CTX))
        x1_d = dram("x1_d", (P, KT, SEQ))
        x2_d = dram("x2_d", (P, KT, SEQ))
        bias_d = dram("bias_d", (16 * P * 384 + 384,))

        raw_landed = [sem(f"raw_landed{n}") for n in range(2)]
        hi_done = sem("hi_done")
        lo_done = sem("lo_done", 2)
        tile_done = sem("tile_done", 2)
        acc_free = sem("acc_free", 2)
        mraw_landed = [sem(f"mraw_landed{n}") for n in range(2)]
        mod_used = sem("mod_used", 2)
        macc_ready = sem("macc_ready")
        mod_out = sem("mod_out", 1)
        mod_red = sem("mod_red")
        pool_step = sem("pool_step")
        consts = sem("consts")
        setup_act = sem("setup_act")
        setup_dve = sem("setup_dve")
        setup_pe = sem("setup_pe")
        bias_st = sem("bias_st")
        x_land = sem("x_land")
        hhi_done = sem("hhi_done")
        hlo_done = sem("hlo_done")
        dve_phase = sem("dve_phase")
        conv_done = sem("conv_done", 1)
        box_ready = sem("box_ready")
        box_mm = sem("box_mm")
        pool_w_land = sem("pool_w_land")
        qk_ready = sem("qk_ready", 1)
        gate_used = sem("gate_used", 1)
        s_ready = sem("s_ready", 4)
        nb_ready = sem("nb_ready")
        exp_done = sem("exp_done", 4)
        a_ready = sem("a_ready")
        t_done = sem("t_done")
        at_evac = sem("at_evac", 4)
        pv_done = sem("pv_done", 1)
        osq_done = sem("osq_done")
        ms_done = sem("ms_done")
        var_ready = sem("var_ready", 1)
        sd_done = sem("sd_done")
        y_done = sem("y_done", 1)
        vt_done = sem("vt_done", 1)
        vt_evac = sem("vt_evac", 1)
        k_st = sem("k_st")
        v_st = sem("v_st")
        k_ld = sem("k_ld")
        v_ld = sem("v_ld")
        xin_land = [sem(f"xin_land{n}") for n in range(2)]
        r_done = sem("r_done", 4)
        mean_done = sem("mean_done")
        d_ready = sem("d_ready")
        sq_ready = sem("sq_ready")
        sq_used = sem("sq_used", 2)
        ln_var = sem("ln_var")
        ln_sd = sem("ln_sd")
        n_ready = sem("n_ready")
        x_ready = sem("x_ready")
        x_st = sem("x_st")
        b_ld = sem("b_ld")
        b_used = sem("b_used", 1)
        s2_ready = sem("s2_ready")
        m2_ready = sem("m2_ready")
        e2_done = sem("e2_done")
        p2_ready = sem("p2_ready")
        t2_done = sem("t2_done")
        t2_evac = sem("t2_evac", 2)
        pv2_done = sem("pv2_done", 1)
        u2_ready = sem("u2_ready", 2)
        th_done = sem("th_done")
        pw_done = sem("pw_done")
        ypw_done = sem("ypw_done", 2)
        pool_done = sem("pool_done", 1)
        y2_done = sem("y2_done", 1)
        gs_done = sem("gs_done", 1)
        rsum_ready = sem("rsum_ready")

        def shown(s, n):
            n = (n if isinstance(n, At) else At(n)) + credits[id(s)]
            assert n.c > 0 or n.k, "a wait for nothing"
            return n.val

        def grant(eng, *sems):
            for s in sems:
                eng.sem_inc(s, credits[id(s)])

        def vec(name, c=0, n=1):
            a = VEC_AT[name]
            return vecs[:, bass.ds(c + a, n)]

        def mod(which, what, m):
            return modc[:, bass.ds(m + (48 * which + 16 * what), 1)]

        def tile(t, k, T):
            return t[:, bass.ds(k * SEQ, T)]

        def loop(eng, first, last, body):
            with eng.Fori(first, last) as i:
                body(i)

        PASS = {"c": 0, "a": 1, "b": 2}
        TOK = {"c": CTX, "a": SEQ, "b": SEQ}
        N0 = {"c": 0, "a": 2 * N_HEADS, "b": 2 * N_HEADS + 4 * N_HEADS}
        H_AT = {"c.h": 0, "c.y": 16, "a.h": 32, "a.y": 48, "kv1": 64, "b.h": 80, "b.y": 96, "g.h": 112,
                "pw": 128, "g.y": 136}
        DVE_PHASES = ["setup", "cconv", "chead", "cpool", "cout", "aconv", "ahead", "apool", "aout", "kv1",
                      "bconv", "bhead", "bpool", "bout", "glu", "kv2", "attn2", "gconv", "pw", "out2"]
        LN_AT = {"c": 0, "a": 16, "b": 32, "cln": 48, "g": 56}
        LN_NO = {"c": 0, "a": 1, "b": 2, "cln": 3, "g": 4}
        VT0 = {"c": 0, "a": 8, "kv1": 16, "b": 24, "kv2": 32}
        CONV0 = {"c": 0, "a": 4, "b": 8, "glu": 12}
        R_AT = {"c": 0, "a": 16, "b": 32, "g": 48}

        def after(phase):
            return DVE_PHASES.index(phase) + 1

        def j_at(phase, i, p=0):
            t = {n: t for n, _, t in STREAM}[phase]
            return At(TILE0[phase] + p, t, i)

        def a_at(phase, i, p=0):
            if phase == "pw":
                return At(TILE0["pw"] + p, 4, i)
            return j_at(phase, i, p) + (4 if phase == "out2" else 0)

        def chunk_at(phase, i, p=0):
            return At(CHUNK0[phase] + p, {n: t for n, _, t in MODS}[phase], i)

        block = ctx.enter_context(nc.Block())

        @block.sync
        def _(sp):
            def load(j, src):
                sp.wait_ge(lo_done, shown(lo_done, j - 1))
                sp.dma_start(raw[:, j.odd * D:(j.odd + 1) * D], src).then_inc(raw_landed[j.odd], 16)

            def stream(phase, w, t0):
                n_iter, tiles = {n: (i, t) for n, i, t in STREAM}[phase]

                def body(i):
                    for p in range(tiles):
                        load(j_at(phase, i, p), w[bass.ds(i * tiles + (t0 + p), 1)])
                if n_iter == 1:
                    body(0)
                else:
                    loop(sp, 0, n_iter, body)

            w0, w1, w2 = A["w0"], A["w1"], A["w2"]
            for c in "ca":
                for phase, t0 in (("conv", 0), ("head", 16), ("pool", 48), ("out", 56)):
                    stream(c + phase, w0, t0)

            def kv(i):
                for p, t in ((0, 18), (1, 17)):
                    load(j_at("kv1", i, p), w1[bass.ds(i * 4 + t, 1)])
            loop(sp, 0, N_HEADS, kv)
            for phase, t0 in (("conv", 0), ("head", 16), ("pool", 48), ("out", 56)):
                stream("b" + phase, w1, t0)
            at = 0
            for phase in ("glu", "kv2", "attn2", "gconv", "pw", "out2"):
                stream(phase, w2, at)
                n, i, t = [s for s in STREAM if s[0] == phase][0]
                at += i * t


        @block.gpsimd
        def _(pool):
            def mods(phase, i, part=slice(None)):
                n = {a: c for a, _, c in MODS}[phase]
                sets, col = MOD_OF[phase]
                first = 24 * MOD_LAYER[sets[0]] + col // 2
                for t in range(n * MOD_TILES)[part]:
                    m = chunk_at(phase, i).times(MOD_TILES) + t
                    pool.wait_ge(mod_used, shown(mod_used, m - 1))
                    pool.sem_inc(pool_step, 1)
                    pool.dma_start(mraw[:, m.odd * 4 * MC:(m.odd + 1) * 4 * MC],
                                   A["wm"][bass.ds(i * (n * MOD_TILES) + (first * MOD_TILES + t), 1)])\
                        .then_inc(mraw_landed[m.odd], 16)

            def head_step(c):
                def step(i, attn=True):
                    if c + "head" in CHUNK0:
                        mods(c + "head", i)
                    if c == "c":
                        pool.wait_ge(qk_ready, shown(qk_ready, At(1, 1, i)))
                        pool.sem_inc(pool_step, 1)
                        pool.dma_start(k_ctx[0][bass.ds(i, 1)], kb[:, 0:CTX]).then_inc(k_st, 16)
                        pool.wait_ge(vt_evac, shown(vt_evac, At(1, 1, i)))
                        pool.sem_inc(pool_step, 1)
                        pool.dma_start(v_ctx[0][bass.ds(i, 1)], vtok[:, 0:CTX]).then_inc(v_st, 16)
                        return
                    l = PASS[c] - 1
                    if attn:
                        pool.wait_ge(s_ready, shown(s_ready, At(N0[c], 4, i)))
                        pool.sem_inc(pool_step, 1)
                    pool.dma_start(kb[:, SEQ:SEQ + CTX], k_ctx[l][bass.ds(i, 1)]).then_inc(k_ld, 16)
                    if attn:
                        pool.wait_ge(pv_done, shown(pv_done, At(8 * PASS[c], 1, i)))
                        pool.sem_inc(pool_step, 1)
                    pool.dma_start(vtok[:, SEQ:SEQ + CTX], v_ctx[l][bass.ds(i, 1)]).then_inc(v_ld, 16)
                step(0, attn=False)
                loop(pool, 1, N_HEADS, step)

            def pool_weights(l, phase):
                pool.wait_ge(dve_phase, shown(dve_phase, after(phase)))
                pool.dma_start(work[:, POOLW:POOLW + 512], A["pool_w"][l]).then_inc(pool_w_land, 16)

            def residual(c, phase, x):
                T = TOK.get(c, SEQ)

                def body(i):
                    for p in range(4):
                        if phase in CHUNK0:
                            mods(phase, i, slice(2 * p, 2 * p + 2))
                        pool.wait_ge(r_done, shown(r_done, At(R_AT[c] + p - 1, 4, i)))
                        pool.sem_inc(pool_step, 1)
                        pool.dma_start((qb, kb)[p % 2][:, 0:T],
                                       x[:, bass.ds(i * 4 + p, 1), :]).then_inc(xin_land[p % 2], 16)
                loop(pool, 0, 4, body)

            def store(c, dst, count):
                pool.wait_ge(x_ready, shown(x_ready, count))
                pool.dma_start(dst, xy3[:, :, 0:TOK.get(c, SEQ)]).then_inc(x_st, 16)

            for dst, src in ((vecs[:], A["vecs"]), (ident[:], A["ident"]), (rope[:], A["rope"]),
                             (edge[:], A["edge"]), (work[:, 0:512], A["lam"].partition_broadcast(P)),
                             (sink[:], A["sinks"].partition_broadcast(P)),
                             (work[0:32, 512:528], A["rel_bias"]), (work[0:32, 528:912], A["onehot"]),
                             (work[0:16, 912:1296], A["negmask"]), (xy3[:, :, 0:CTX], A["ctxT"])):
                pool.dma_start(dst, src).then_inc(consts, 16)
            loop(pool, 0, 8, lambda i: mods("mod0", i))
            pool.wait_ge(setup_dve, shown(setup_dve, 3))
            pool.dma_start(bias_d[0:16 * P * 384].rearrange("(h q n) -> h q n", q=P, n=384),
                           work[0:16, 912:1296].unsqueeze(1).broadcast_to([16, P, 384])).then_inc(bias_st, 16)
            head_step("c")
            pool_weights(0, "chead")
            pool.wait_ge(dve_phase, shown(dve_phase, after("cpool")))
            residual("c", "cout", A["ctxT"])
            store("c", c1_d, 16)
            pool.wait_ge(x_st, shown(x_st, 16))
            pool.dma_start(xy3, A["xT"]).then_inc(x_land, 16)
            pool.wait_ge(k_st, shown(k_st, 16 * N_HEADS))
            pool.wait_ge(v_st, shown(v_st, 16 * N_HEADS))
            pool.wait_ge(dve_phase, shown(dve_phase, after("aconv")))
            head_step("a")
            pool_weights(0, "ahead")
            pool.wait_ge(dve_phase, shown(dve_phase, after("apool")))
            pool.dma_start(work[:, 0:KT * CTX].rearrange("p (k t) -> p k t", t=CTX), c1_d).then_inc(x_land, 16)
            residual("a", "aout", A["xT"])

            def kv1_store(i):
                pool.wait_ge(acc_free, shown(acc_free, a_at("kv1", i, 1) + 1))
                pool.sem_inc(pool_step, 1)
                pool.dma_start(k_ctx[1][bass.ds(i, 1)], kb[:, 0:CTX]).then_inc(k_st, 16)
                pool.wait_ge(vt_evac, shown(vt_evac, At(VT0["kv1"] + 1, 1, i)))
                pool.sem_inc(pool_step, 1)
                pool.dma_start(v_ctx[1][bass.ds(i, 1)], vtok[:, 0:CTX]).then_inc(v_st, 16)
            loop(pool, 0, N_HEADS, kv1_store)
            store("a", x1_d, 32)
            loop(pool, 0, 4, lambda i: mods("bconv", i))
            pool.wait_ge(k_st, shown(k_st, 2 * 16 * N_HEADS))
            pool.wait_ge(v_st, shown(v_st, 2 * 16 * N_HEADS))
            pool.wait_ge(x_st, shown(x_st, 32))
            pool.wait_ge(dve_phase, shown(dve_phase, after("bconv")))
            head_step("b")
            pool_weights(1, "bhead")
            pool.wait_ge(dve_phase, shown(dve_phase, after("bpool")))
            residual("b", "bout", x1_d)
            store("b", x2_d, 48)
            pool.wait_ge(bias_st, shown(bias_st, 16))
            pool.wait_ge(dve_phase, shown(dve_phase, after("kv2")))

            def biases(i):
                pool.wait_ge(b_used, shown(b_used, At(0, 1, i)))
                pool.sem_inc(pool_step, 1)
                for e in range(2):
                    rows = bass.AP(bias_d.tensor, i * (2 * P * 384) + (e * P * 384 + BLOCK - 1), [[383, P], [1, 256]])
                    pool.dma_start(ev[1][:, 256 * e:256 * e + 256], rows).then_inc(b_ld, 16)
            loop(pool, 0, 8, biases)
            pool.wait_ge(x_st, shown(x_st, 48))
            pool.wait_ge(dve_phase, shown(dve_phase, after("pw")))
            residual("g", "out2", x2_d)
            store("g", out, 64)
            pool.wait_ge(x_st, shown(x_st, 64))

        @block.scalar
        def _(act):
            def f(out, in_, func=ACT.Copy, **kw):
                return nc.scalar.activation(out, in_, func, **kw)

            def hi(j):
                act.wait_ge(raw_landed[j.odd], shown(raw_landed[j.odd], j.half.times(16) + 16))
                act.wait_ge(tile_done, shown(tile_done, j - 1))
                f(w_hi[:, j.odd * D:(j.odd + 1) * D], raw[:, j.odd * D:(j.odd + 1) * D]).then_inc(hi_done, 1)

            def modulate(c, which, src, T):
                def body(i):
                    f(tile(h_hi, i, T), src(i), ACT.Identity, scale=mod(which, 1, i),
                      bias=mod(which, 0, i)).then_inc(hhi_done, 1)
                loop(act, 0, KT, body)

            def split_y(T, count=KT, base=0):
                loop(act, 0, count, lambda i: f(tile(h_hi, i, T), tile(xy, i + base, T)).then_inc(hhi_done, 1))

            def half_and_tanh(x, half, th):
                f(half, x, ACT.Copy, scale=0.5)
                return f(th, x, ACT.Tanh, scale=0.5)

            def conv(c):
                T, phase = TOK[c], c + "conv"

                def body(g):
                    for p in range(4):
                        j, a = j_at(phase, g, p), a_at(phase, g, p)
                        hi(j + 1)
                        x = acc[a.odd][:, 0:T]
                        if p == 0:
                            act.wait_ge(conv_done, shown(conv_done, At(CONV0[c], 1, g)))
                        act.wait_ge(tile_done, shown(tile_done, j + 1))
                        if p < 3:
                            f(ev[p][:, 0:T], x).then_inc(acc_free, 1)
                        else:
                            half_and_tanh(x, ev[3][:, 0:T], evt[:, 0:T]).then_inc(acc_free, 1)
                loop(act, 0, N_CONV, body)

            def heads(c):
                T, phase, h0 = TOK[c], c + "head", 8 * PASS[c]
                QT = T // P
                NK = T + (CTX if c != "c" else 0)

                def step(i, proj=True, attn=True):
                    for p in range(4):
                        j, a = j_at(phase, i, p), a_at(phase, i, p)
                        n = At(N0[c] - QT + p, QT, i)
                        if proj:
                            hi(j + 1)
                        if attn and p < QT:
                            act.wait_ge(nb_ready, shown(nb_ready, n + 1))
                            act.wait_ge(t_done, shown(t_done, n))
                            for m in range(2):
                                e = f(maps[m][:, 0:NK], S[:, 1024 * m:1024 * m + NK], ACT.Exp,
                                      bias=small[:, m:m + 1], accum_out=small[:, 2 + m:3 + m])
                            e.then_inc(exp_done, 1)
                        if proj:
                            x = acc[a.odd][:, 0:T]
                            if p == 0:
                                act.wait_ge(qk_ready, shown(qk_ready, At(h0, 1, i)))
                            if p == 2:
                                act.wait_ge(vt_done, shown(vt_done, At(VT0[c], 1, i)))
                            if p == 3:
                                act.wait_ge(gate_used, shown(gate_used, At(h0, 1, i)))
                            act.wait_ge(tile_done, shown(tile_done, j + 1))
                            if p == 0:
                                f(ev[0][:, 0:T], x, scale=QK ** -0.5).then_inc(acc_free, 1)
                            elif p < 3:
                                f(ev[p][:, 0:T], x).then_inc(acc_free, 1)
                            else:
                                half_and_tanh(x, ev[3][:, 0:T], evt[:, 0:T]).then_inc(acc_free, 1)
                        if attn and p < QT:
                            act.wait_ge(t_done, shown(t_done, n + 1))
                            if p == 0:
                                act.wait_ge(pv_done, shown(pv_done, At(h0 - 1, 1, i)))
                            f(a_t[:, 0:NK // P * T].rearrange("p (k t) -> p k t", t=T)[:, :, P * p:P * (p + 1)],
                              S[:, 0:NK].rearrange("p (k q) -> p k q", q=P)).then_inc(at_evac, 1)
                    if attn:
                        act.wait_ge(pv_done, shown(pv_done, At(h0, 1, i)))
                        f(maps[1][:, 0:T], pv[:, 0:T], ACT.Square).then_inc(osq_done, 1)
                    if proj:
                        act.wait_ge(vt_done, shown(vt_done, At(VT0[c] + 1, 1, i)))
                        if c == "c" and attn:
                            act.wait_ge(v_st, shown(v_st, At(0, 16, i)))
                        f(vtok[:, 0:T], misc[:, 0:T]).then_inc(vt_evac, 1)
                    if attn:
                        act.wait_ge(var_ready, shown(var_ready, At(h0, 1, i)))
                        f(t2[:, 0:T], t2[:, 0:T], ACT.Sqrt).then_inc(sd_done, 1)
                act.wait_ge(dve_phase, shown(dve_phase, after(c + "conv")))
                step(0, attn=False)
                loop(act, 1, N_HEADS, step)
                step(N_HEADS, proj=False)

            def pooling(c):
                T, phase = TOK[c], c + "pool"
                act.wait_ge(dve_phase, shown(dve_phase, after(c + "head")))

                def group(g):
                    for p in range(2):
                        j, a = j_at(phase, g, p), a_at(phase, g, p)
                        hi(j + 1)
                        x = acc[a.odd][:, 0:T]
                        act.wait_ge(pool_done, shown(pool_done, 4 * PASS[c] + g))
                        act.wait_ge(tile_done, shown(tile_done, j + 1))
                        if p == 0:
                            f(ev[0][:, 0:T], x).then_inc(acc_free, 1)
                        else:
                            half_and_tanh(x, ev[3][:, 0:T], evt[:, 0:T]).then_inc(acc_free, 1)
                for g in range(N_POOL):
                    group(g)

            def project_out(c, phase, which):
                T = TOK.get(c, SEQ)

                def body(i, last=False):
                    for p in range(4):
                        j, a = j_at(phase, i, p), a_at(phase, i, p)
                        if not (last and p == 3):
                            hi(j + 1)
                        act.wait_ge(r_done, shown(r_done, At(R_AT[c] + p - 3, 4, i)))
                        act.wait_ge(tile_done, shown(tile_done, j + 1))
                        f(ev[p][:, 0:T], acc[a.odd][:, 0:T], scale=mod(which, 2, i * 4 + p)).then_inc(acc_free, 1)
                if phase == "out2":
                    loop(act, 0, 3, body)
                    body(3, last=True)
                else:
                    loop(act, 0, 4, body)

            def norm(c, T, base, count):
                at = LN_AT[c]

                def body(i):
                    for s in range(2):
                        act.wait_ge(d_ready, shown(d_ready, At(at + s + 1, 2, i)))
                        act.wait_ge(sq_used, shown(sq_used, At(at + s - 1, 2, i)))
                        f(ev[s][:, 0:T], tile(xy, i * 2 + (base + s), T), ACT.Square).then_inc(sq_ready, 1)
                loop(act, 0, count // 2, body)
                act.wait_ge(ln_var, shown(ln_var, LN_NO[c] + 1))
                f(t1[:, 0:T], t1[:, 0:T], ACT.Sqrt).then_inc(ln_sd, 1)

            def norm_affine(c, T, layer):
                def body(i):
                    act.wait_ge(n_ready, shown(n_ready, At(LN_AT[c] + 1, 1, i)))
                    f(tile(xy, i, T), tile(xy, i, T), ACT.Identity, scale=vec(f"ln_g{layer}", i),
                      bias=vec(f"ln_b{layer}", i)).then_inc(x_ready, 1)
                loop(act, 0, KT, body)

            grant(act, acc_free, exp_done, at_evac, vt_evac, t2_evac)
            act.wait_ge(consts, shown(consts, 160))
            f(t1[:, 0:48], vec("c0", 0, 48), ACT.Tanh, scale=0.5).then_inc(setup_act, 1)
            act.wait_ge(setup_dve, shown(setup_dve, 2))
            f(small[:, 4:8], small[:, 0:4], ACT.Exp).then_inc(setup_act, 1)
            act.wait_ge(dve_phase, shown(dve_phase, after("setup")))
            hi(At(0))
            modulate("c.h", 1, lambda i: tile(xy, i, CTX), CTX)
            for c, layer, l in (("c", 0, 0), ("a", 0, 0), ("b", 2, 1)):
                T = TOK[c]
                which = {"c": 1, "a": 0, "b": 2}[c]
                if c == "a":
                    act.wait_ge(x_land, shown(x_land, 16))
                    act.wait_ge(tile_done, shown(tile_done, TILE0["aconv"]))
                    modulate("a.h", 0, lambda i: tile(xy, i, SEQ), SEQ)
                if c == "b":
                    act.wait_ge(tile_done, shown(tile_done, TILE0["bconv"]))
                    act.drain()
                    modulate("b.h", 2, lambda i: tile(xy, i, SEQ), SEQ)
                conv(c)
                heads(c)
                pooling(c)
                act.wait_ge(dve_phase, shown(dve_phase, after(c + "pool")))
                act.wait_ge(tile_done, shown(tile_done, TILE0[c + "out"]))
                split_y(T)
                project_out(c, c + "out", which)
                if c == "a":
                    act.wait_ge(x_land, shown(x_land, 32))
                    act.wait_ge(tile_done, shown(tile_done, TILE0["kv1"]))
                    modulate("kv1", 3, lambda i: work[:, bass.ds(i * CTX, CTX)], CTX)

                    def kv1(i):
                        for p in range(2):
                            j, a = j_at("kv1", i, p), a_at("kv1", i, p)
                            hi(j + 1)
                            if p == 0:
                                act.wait_ge(vt_done, shown(vt_done, At(VT0["kv1"], 1, i)))
                                act.wait_ge(r_done, shown(r_done, 32))
                            else:
                                act.wait_ge(k_st, shown(k_st, At(16 * N_HEADS, 16, i)))
                            act.wait_ge(tile_done, shown(tile_done, j + 1))
                            f((ev[2], kb)[p][:, 0:CTX], acc[a.odd][:, 0:CTX]).then_inc(acc_free, 1)
                        act.wait_ge(vt_done, shown(vt_done, At(VT0["kv1"] + 1, 1, i)))
                        act.wait_ge(v_st, shown(v_st, At(16 * N_HEADS, 16, i)))
                        f(vtok[:, 0:CTX], misc[:, 0:CTX]).then_inc(vt_evac, 1)
                    loop(act, 0, N_HEADS, kv1)
                norm(c, T, 0, KT)
                norm_affine(c, T, l)
            act.wait_ge(tile_done, shown(tile_done, TILE0["glu"]))
            act.drain()
            modulate("g.h", 4, lambda i: tile(xy, i, SEQ), SEQ)

            def glu(c):
                for p in range(2):
                    j, a = j_at("glu", c, p), a_at("glu", c, p)
                    hi(j + 1)
                    act.wait_ge(conv_done, shown(conv_done, At(CONV0["glu"], 1, c)))
                    act.wait_ge(tile_done, shown(tile_done, j + 1))
                    x = acc[a.odd][:, :]
                    (f(ev[0][:], x, scale=0.5) if p == 0 else f(evt[:], x, ACT.Tanh, scale=0.5)).then_inc(acc_free, 1)
            loop(act, 0, 8, glu)
            norm("cln", SEQ, 8, 8)

            def conv_silu(i):
                for s in range(2):
                    act.wait_ge(n_ready, shown(n_ready, At(LN_AT["cln"] + s + 1, 2, i)))
                    act.wait_ge(u2_ready, shown(u2_ready, At(s - 1, 2, i)))
                    u = tile(xy, i * 2 + (8 + s), SEQ)
                    f(u, u, ACT.Identity, scale=vec("cln_g", i * 2 + s), bias=vec("cln_b", i * 2 + s))
                    act.drain()
                    f(ev[s][:], u, ACT.Tanh).then_inc(th_done, 1)
            loop(act, 0, 4, conv_silu)
            for p in range(4):
                j, a = j_at("kv2", 0, p), a_at("kv2", 0, p)
                hi(j + 1)
                if p == 2:
                    act.wait_ge(dve_phase, shown(dve_phase, after("glu")))
                act.wait_ge(tile_done, shown(tile_done, j + 1))
                f((k2[:, 0:512], k2[:, 512:1024], ev[0][:], ev[1][:])[p], acc[a.odd][:, :]).then_inc(acc_free, 1)
            for v in range(2):
                act.wait_ge(vt_done, shown(vt_done, VT0["kv2"] + v + 1))
                f(vtok[:, :].rearrange("p (b n) -> p b n", b=4)[:, :, P * v:P * (v + 1)],
                  misc[:, :].rearrange("p (b n) -> p b n", b=4)).then_inc(vt_evac, 1)

            def attn2(i, proj=True, attn=True):
                for p in range(2):
                    j, a = j_at("attn2", i, p), a_at("attn2", i, p)
                    if proj:
                        hi(j + 1)
                    if attn and p == 0:
                        for e in range(2):
                            act.wait_ge(m2_ready, shown(m2_ready, At(e - 1, 2, i)))
                            o = 8 + 12 * e
                            for b in range(4):
                                s = s2[e][:, 256 * b + (P if b == 0 else 0):256 * (b + 1)]
                                f(s, s, ACT.Exp, bias=small[:, o + b:o + b + 1],
                                  accum_out=small[:, o + 4 + b:o + 5 + b])
                            f(small[:, o + 8:o + 12], small[:, o:o + 4], ACT.Exp,
                              bias=sink[:, bass.ds(i * 2 + (e - 2), 1)]).then_inc(e2_done, 1)
                    if attn and p == 1:
                        for e in range(2):
                            act.wait_ge(t2_done, shown(t2_done, At(e - 1, 2, i)))
                            f(s2[e][:, P:1024], S[:, 1024 * e + P:1024 * (e + 1)]).then_inc(t2_evac, 1)
                    if proj:
                        if p == 1:
                            act.wait_ge(gate_used, shown(gate_used, At(24, 1, i)))
                        act.wait_ge(tile_done, shown(tile_done, j + 1))
                        if p == 0:
                            f(qb[:], acc[a.odd][:, :], scale=QK ** -0.5).then_inc(acc_free, 1)
                        else:
                            half_and_tanh(acc[a.odd][:, :], ev[3][:], evt[:]).then_inc(acc_free, 1)
            attn2(0, attn=False)
            loop(act, 1, 8, attn2)
            attn2(8, proj=False)

            def gconv(i):
                for p in range(2):
                    j, a = j_at("gconv", i, p), a_at("gconv", i, p)
                    hi(j + 1)
                    act.wait_ge(dve_phase, shown(dve_phase, after("attn2")))
                    act.wait_ge(gs_done, shown(gs_done, At(0, 1, i)))
                    act.wait_ge(tile_done, shown(tile_done, j + 1))
                    half_and_tanh(acc[a.odd][:, :], ev[2 * p][:], ev[2 * p + 1][:]).then_inc(acc_free, 1)
            loop(act, 0, 4, gconv)
            act.wait_ge(tile_done, shown(tile_done, TILE0["pw"]))
            split_y(SEQ, 8, 8)

            def pw(i):
                for t in range(2):
                    j = j_at("pw", i, t)
                    hi(j + 1)
                    for s in range(2):
                        m = 2 * t + s
                        a = a_at("pw", i, m)
                        act.wait_ge(dve_phase, shown(dve_phase, after("gconv")))
                        act.wait_ge(ypw_done, shown(ypw_done, At(m - 1, 4, i)))
                        if s == 0:
                            act.wait_ge(pw_done, shown(pw_done, At(t + 1, 2, i)))
                        else:
                            act.wait_ge(tile_done, shown(tile_done, j + 1))
                        f(ev[s][:], acc[a.odd][:, :], ACT.Identity,
                          bias=vec("b_pw", i * 4 + m)).then_inc(acc_free, 1)
            loop(act, 0, 2, pw)
            act.wait_ge(dve_phase, shown(dve_phase, after("pw")))
            act.wait_ge(tile_done, shown(tile_done, TILE0["out2"]))
            split_y(SEQ)
            project_out("g", "out2", 4)
            norm("g", SEQ, 0, KT)
            norm_affine("g", SEQ, 2)

        @block.tensor
        def _(pe):
            mm = nc.tensor.matmul

            def product(o, j, a, ks, w_k0=0):
                for n, k in enumerate(ks):
                    w = slice(j.odd * D + (w_k0 + n) * P, j.odd * D + (w_k0 + n + 1) * P)
                    T = o.shape[1]
                    x = slice(k * SEQ, k * SEQ + T)
                    mm(o, w_hi[:, w], h_hi[:, x], start=n == 0, stop=False)
                    mm(o, w_hi[:, w], h_lo[:, x], start=False, stop=False)
                    last = mm(o, w_lo[:, w], h_hi[:, x], start=False, stop=n == len(ks) - 1)
                return last

            def weight_tile(j, a, T, h):
                pe.wait_ge(hlo_done, shown(hlo_done, h))
                pe.wait_ge(lo_done, shown(lo_done, j + 1))
                pe.wait_ge(acc_free, shown(acc_free, a - 1))
                product(acc[a.odd][:, 0:T], j, a, range(KT)).then_inc(tile_done, 1)

            def reduce_mod(phase, i, c):
                q = chunk_at(phase, i, c)
                par = c
                pe.wait_ge(macc_ready, shown(macc_ready, q + 1))
                pe.wait_ge(mod_out, shown(mod_out, q))
                nv = len(MOD_OF[phase][0])
                for v in range(nv):
                    for s in range(2):
                        at = (par * 2 + v) * MC + s * P
                        last = mm(mod_ps[:, 2 * v + s:2 * v + s + 1], macc[:, at:at + P], ones[:, 0:1],
                                  start=True, stop=True)
                last.then_inc(mod_red, 1)

            def conv(c):
                phase = c + "conv"

                def body(g):
                    for p in range(4):
                        weight_tile(j_at(phase, g, p), a_at(phase, g, p), TOK[c], H_AT[c + ".h"] + KT)
                        if phase in CHUNK0 and p >= 2:
                            reduce_mod(phase, g, p - 2)
                loop(pe, 0, N_CONV, body)

            def heads(c):
                T, phase, h0 = TOK[c], c + "head", 8 * PASS[c]
                QT = T // P
                LT = T // P
                ctx_keys = CTX if c != "c" else 0
                NK = T + ctx_keys

                def scores(i, qt):
                    n = At(N0[c] - QT + qt, QT, i)
                    if qt == 0:
                        pe.wait_ge(qk_ready, shown(qk_ready, At(h0, 1, i)))
                        pe.wait_ge(var_ready, shown(var_ready, At(h0 - 1, 1, i)))
                        if ctx_keys:
                            pe.wait_ge(k_ld, shown(k_ld, At(16 * (h0 - 8), 16, i)))
                    pe.wait_ge(exp_done, shown(exp_done, n))
                    pe.wait_ge(at_evac, shown(at_evac, n))
                    for m in range(2):
                        h = slice(QK * m, QK * (m + 1))
                        q = qb[h, P * qt:P * (qt + 1)]
                        last = mm(S[:, 1024 * m:1024 * m + T], q, kb[h, 0:T], start=True, stop=True)
                        if ctx_keys:
                            last = mm(S[:, 1024 * m + T:1024 * m + NK], q, kb[h, T:NK], start=True, stop=True)
                    last.then_inc(s_ready, 1)

                def transposes(i, qt):
                    pe.wait_ge(a_ready, shown(a_ready, At(N0[c] - QT + qt + 1, QT, i)))
                    for k in range(NK // P):
                        last = nc.tensor.transpose(S[:, P * k:P * (k + 1)], maps[0][:, P * k:P * (k + 1)], ident[:])
                    last.then_inc(t_done, 1)

                def step(i, proj=True, attn=True):
                    if attn:
                        scores(i, 0)
                    for p in range(4):
                        if proj:
                            weight_tile(j_at(phase, i, p), a_at(phase, i, p), T, H_AT[c + ".h"] + KT)
                        if attn and p < QT:
                            transposes(i, p)
                            if p + 1 < QT:
                                scores(i, p + 1)
                        if proj and phase in CHUNK0 and p == 2 and c != "c":
                            pe.wait_ge(vt_evac, shown(vt_evac, At(VT0[c], 1, i)))
                            reduce_mod(phase, i, 0)
                    if attn:
                        pe.wait_ge(at_evac, shown(at_evac, At(N0[c], QT, i)))
                        pe.wait_ge(vt_evac, shown(vt_evac, At(VT0[c], 1, i)))
                        pe.wait_ge(y_done, shown(y_done, At(h0 - 1, 1, i)))
                        if ctx_keys:
                            pe.wait_ge(v_ld, shown(v_ld, At(16 * (h0 - 8), 16, i)))
                        for k in range(NK // P):
                            last = mm(pv[:, 0:T], vtok[:, P * k:P * (k + 1)], a_t[:, k * T:(k + 1) * T],
                                      start=k == 0, stop=k == NK // P - 1)
                        last.then_inc(pv_done, 1)
                    if proj:
                        pe.wait_ge(acc_free, shown(acc_free, a_at(phase, i, 2) + 1))
                        pe.wait_ge(vt_evac, shown(vt_evac, At(VT0[c], 1, i)))
                        if phase in CHUNK0:
                            pe.wait_ge(mod_out, shown(mod_out, chunk_at(phase, i, 0) + (1 if c != "c" else 0)))
                        for t in range(LT):
                            last = nc.tensor.transpose(misc[:, P * t:P * (t + 1)], ev[2][:, P * t:P * (t + 1)], ident[:])
                        last.then_inc(vt_done, 1)
                    if attn:
                        pe.wait_ge(osq_done, shown(osq_done, At(h0, 1, i)))
                        mm(S[:, 1024:1024 + T], ones[:], maps[1][:, 0:T], start=True, stop=True).then_inc(ms_done, 1)
                    if proj and phase in CHUNK0:
                        pe.wait_ge(vt_evac, shown(vt_evac, At(VT0[c] + 1, 1, i)))
                        reduce_mod(phase, i, 0 if c == "c" else 1)
                step(0, attn=False)
                loop(pe, 1, N_HEADS, step)
                step(N_HEADS, proj=False)

            def pooling(c):
                T, phase = TOK[c], c + "pool"
                pe.wait_ge(pool_w_land, shown(pool_w_land, 16 * (PASS[c] + 1)))

                def mix(g):
                    pe.wait_ge(box_ready, shown(box_ready, 4 * PASS[c] + g + 1))
                    pe.wait_ge(pool_done, shown(pool_done, 4 * PASS[c] + g))
                    mm(pv[:, 0:T], work[:, POOLW + P * g:POOLW + P * (g + 1)], work[:, 1584:1584 + T],
                       start=True, stop=True).then_inc(box_mm, 1)
                pe.wait_ge(y_done, shown(y_done, 8 * (PASS[c] + 1)))
                for g in range(N_POOL):
                    for p in range(2):
                        weight_tile(j_at(phase, g, p), a_at(phase, g, p), T, H_AT[c + ".h"] + KT)
                    mix(g)

            def project_out(c, phase):
                T = TOK.get(c, SEQ)

                def body(i):
                    for p in range(4):
                        weight_tile(j_at(phase, i, p), a_at(phase, i, p), T, H_AT[c + ".y"] + KT)
                        if phase in CHUNK0 and p >= 2:
                            reduce_mod(phase, i, p - 2)
                loop(pe, 0, 4, body)

            def norm(c, T, count):
                pe.wait_ge(rsum_ready, shown(rsum_ready, LN_NO[c] + 1))
                mm(pv[:, 0:T], ones[:], t1[:, 0:T], start=True, stop=True).then_inc(mean_done, 1)
                for k in range(count):
                    pe.wait_ge(sq_ready, shown(sq_ready, LN_AT[c] + k + 1))
                    mm(misc[:, 0:T], ones[:], ev[k % 2][:, 0:T], start=k == 0, stop=k == count - 1).then_inc(sq_used, 1)

            grant(pe, tile_done, s_ready, pv_done, vt_done, sq_used, pv2_done)
            pe.wait_ge(consts, shown(consts, 160))
            mm(misc[0:16, 0:384], work[0:32, 512:528], work[0:32, 528:912], start=True, stop=True).then_inc(setup_pe, 1)
            pe.wait_ge(setup_dve, shown(setup_dve, 1))

            def mod0(i):
                for c in range(2):
                    reduce_mod("mod0", i, c)
            loop(pe, 0, 8, mod0)
            for c in "cab":
                conv(c)
                heads(c)
                pooling(c)
                project_out(c, c + "out")
                if c == "a":
                    def kv1(i):
                        for p in range(2):
                            weight_tile(j_at("kv1", i, p), a_at("kv1", i, p), CTX, H_AT["kv1"] + KT)
                        pe.wait_ge(acc_free, shown(acc_free, a_at("kv1", i, 0) + 1))
                        pe.wait_ge(vt_evac, shown(vt_evac, At(VT0["kv1"], 1, i)))
                        for t in range(CTX // P):
                            last = nc.tensor.transpose(misc[:, P * t:P * (t + 1)], ev[2][:, P * t:P * (t + 1)], ident[:])
                        last.then_inc(vt_done, 1)
                    loop(pe, 0, N_HEADS, kv1)
                norm(c, TOK[c], KT)
            h2 = H_AT["g.h"] + KT

            def glu(c):
                for p in range(2):
                    weight_tile(j_at("glu", c, p), a_at("glu", c, p), SEQ, h2)
            loop(pe, 0, 8, glu)
            norm("cln", SEQ, 8)
            for p in range(4):
                weight_tile(j_at("kv2", 0, p), a_at("kv2", 0, p), SEQ, h2)
            for v in range(2):
                pe.wait_ge(acc_free, shown(acc_free, a_at("kv2", 0, 2 + v) + 1))
                pe.wait_ge(vt_evac, shown(vt_evac, VT0["kv2"] + v))
                for b in range(4):
                    last = nc.tensor.transpose(misc[:, P * b:P * (b + 1)], ev[v][:, P * b:P * (b + 1)], ident[:])
                last.then_inc(vt_done, 1)

            def attn2(pair, proj=True, attn=True):
                def step(i):
                    if attn:
                        pe.wait_ge(acc_free, shown(acc_free, a_at("attn2", i, -2) + 1))
                        for e in range(2):
                            pe.wait_ge(t2_evac, shown(t2_evac, At(e - 3, 2, i)))
                            h = slice(QK * e, QK * (e + 1))
                            for b in range(4):
                                k0 = 512 * pair + P * max(b - 1, 0)
                                n = 256 if b else P
                                last = mm(S[:, 1024 * e + 256 * (b + 1) - n:1024 * e + 256 * (b + 1)],
                                          qb[h, P * b:P * (b + 1)], k2[h, k0:k0 + n], start=True, stop=True)
                            last.then_inc(s2_ready, 1)
                    if proj:
                        weight_tile(j_at("attn2", i, 0), a_at("attn2", i, 0), SEQ, h2)
                    if attn:
                        for e in range(2):
                            pe.wait_ge(p2_ready, shown(p2_ready, At(e - 1, 2, i)))
                            for t in range(1, 8):
                                last = nc.tensor.transpose(S[:, 1024 * e + P * t:1024 * e + P * (t + 1)],
                                                           s2[e][:, P * t:P * (t + 1)], ident[:])
                            last.then_inc(t2_done, 1)
                    if proj:
                        weight_tile(j_at("attn2", i, 1), a_at("attn2", i, 1), SEQ, h2)
                    if attn:
                        pe.wait_ge(t2_evac, shown(t2_evac, At(0, 2, i)))
                        pe.wait_ge(y2_done, shown(y2_done, At(-1, 1, i)))
                        for e in range(2):
                            for b in range(4):
                                for x in range(2 if b else 1):
                                    v = 256 * (b - x) + QK * (2 * pair + e)
                                    p = 256 * b + (P if x == 0 else 0)
                                    last = mm(pv[QK * e:QK * (e + 1), P * b:P * (b + 1)], vtok[:, v:v + QK],
                                              s2[e][:, p:p + P], start=x == 0, stop=x == (1 if b else 0))
                        last.then_inc(pv2_done, 1)
                return step
            pe.wait_ge(vt_evac, shown(vt_evac, VT0["kv2"] + 2))
            attn2(0, attn=False)(0)
            loop(pe, 1, 5, attn2(0))
            loop(pe, 5, 8, attn2(1))
            attn2(1, proj=False)(8)

            def gconv(i):
                for p in range(2):
                    weight_tile(j_at("gconv", i, p), a_at("gconv", i, p), SEQ, h2)
            loop(pe, 0, 4, gconv)

            def pw(i):
                for t in range(2):
                    j = j_at("pw", i, t)
                    pe.wait_ge(hlo_done, shown(hlo_done, H_AT["pw"] + 8))
                    pe.wait_ge(lo_done, shown(lo_done, j + 1))
                    for s in range(2):
                        a = a_at("pw", i, 2 * t + s)
                        pe.wait_ge(acc_free, shown(acc_free, a - 1))
                        product(acc[a.odd][:, :], j, a, range(8), 8 * s).then_inc((pw_done, tile_done)[s], 1)
            loop(pe, 0, 2, pw)
            project_out("g", "out2")
            norm("g", SEQ, KT)

        @block.vector
        def _(dve):
            tt, ts, stt = nc.vector.tensor_tensor, nc.vector.tensor_scalar, nc.vector.scalar_tensor_tensor
            phases_done = [0]

            def phase_done(name):
                dve.drain()
                dve.sem_inc(dve_phase, 1)
                assert DVE_PHASES[phases_done[0]] == name, name
                phases_done[0] += 1

            def lo(j):
                dve.wait_ge(hi_done, shown(hi_done, j + 1))
                s = slice(j.odd * D, (j.odd + 1) * D)
                tt(w_lo[:, s], raw[:, s], w_hi[:, s].bitcast(F32), ALU.subtract).then_inc(lo_done, 1)

            def modulate(c, which, src, T, both=(t1, t2)):
                h = H_AT[c]

                def body(i):
                    dve.drain()
                    for s in range(2):
                        ts(both[s][:, 0:T], src(i * 2 + s), mod(which, 1, i * 2 + s), mod(which, 0, i * 2 + s),
                           ALU.mult, ALU.add)
                    dve.drain()
                    for s in range(2):
                        dve.wait_ge(hhi_done, shown(hhi_done, At(h + s + 1, 2, i)))
                        tt(tile(h_lo, i * 2 + s, T), both[s][:, 0:T], tile(h_hi, i * 2 + s, T).bitcast(F32),
                           ALU.subtract).then_inc(hlo_done, 1)
                loop(dve, 0, KT // 2, body)

            def split_y(c, T, count=KT, base=0):
                def body(i):
                    dve.wait_ge(hhi_done, shown(hhi_done, At(H_AT[c] + 1, 1, i)))
                    tt(tile(h_lo, i, T), tile(xy, i + base, T), tile(h_hi, i, T).bitcast(F32),
                       ALU.subtract).then_inc(hlo_done, 1)
                loop(dve, 0, count, body)

            def mod_tiles(phase, i, c, tiles):
                sets, _ = MOD_OF[phase]
                q = chunk_at(phase, i, c)
                par = c
                for t in tiles:
                    m = q.times(MOD_TILES) + t
                    for kk in range(4):
                        k = 4 * t + kk
                        if k:
                            dve.drain()
                        if kk == 0:
                            dve.wait_ge(mraw_landed[m.odd], shown(mraw_landed[m.odd], m.half.times(16) + 16))
                        for v, w in enumerate(sets):
                            s = macc[:, (par * 2 + v) * MC:(par * 2 + v + 1) * MC]
                            x = mraw[:, (m.odd * 4 + kk) * MC:(m.odd * 4 + kk + 1) * MC]
                            cc = csil[:, 16 * MOD_VEC[w] + k:16 * MOD_VEC[w] + k + 1]
                            last = ts(s, x, cc, None, ALU.mult) if k == 0 else stt(s, x, cc, s, ALU.mult, ALU.add)
                    last.then_inc(mod_used, 1)
                if tiles[-1] == MOD_TILES - 1:
                    dve.drain()
                    dve.sem_inc(macc_ready, 1)

            def mod_columns(phase, i, c):
                sets, col = MOD_OF[phase]
                n = {a: n for a, _, n in MODS}[phase]
                dve.wait_ge(mod_red, shown(mod_red, chunk_at(phase, i, c) + 1))
                for v, w in enumerate(sets):
                    m = i * (2 * n) + (2 * c + col)
                    last = tt(modc[:, bass.ds(m + 48 * w, 2)], mod_ps[:, 2 * v:2 * v + 2],
                              vec(f"b_mod{MOD_LAYER[w]}", m, 2), ALU.add)
                last.then_inc(mod_out, 1)

            def one_plus(sets):
                dve.drain()
                for w in sets:
                    s = modc[:, 48 * w + 16:48 * w + 32]
                    ts(s, s, 1.0, None, ALU.add)
                dve.drain()

            def conv(c, l):
                T, phase = TOK[c], c + "conv"
                v = work[:, 0:T + 2]
                y, g = t1[:, 0:T], t2[:, 0:T]
                nc.vector.memset(work[:, 0:1], 0.0)
                nc.vector.memset(work[:, T + 1:T + 2], 0.0)
                dve.drain()

                def body(i):
                    for p in range(4):
                        j, a = j_at(phase, i, p), a_at(phase, i, p)
                        lo(j + 1)
                        if phase in CHUNK0:
                            mod_tiles(phase, i, p // 2, (0, 1) if p % 2 == 0 else (2, 3))
                            if p == 3:
                                mod_columns(phase, i, 0)
                        if p == 2:
                            dve.wait_ge(acc_free, shown(acc_free, a_at(phase, i, 1) + 1))
                            tt(work[:, 1:T + 1], ev[0][:, 0:T], ev[1][:, 0:T], ALU.mult)
                            dve.drain()
                            ts(y, v[:, 0:T], vec(f"conv_w{l}", i), None, ALU.mult)
                            for tap in (1, 2):
                                dve.drain()
                                stt(y, v[:, tap:tap + T], vec(f"conv_w{l}", i + 4 * tap), y, ALU.mult, ALU.add)
                    dve.drain()
                    dve.wait_ge(acc_free, shown(acc_free, a_at(phase, i, 3) + 1))
                    tt(y, y, ev[2][:, 0:T], ALU.mult)
                    stt(g, evt[:, 0:T], 1.0, ev[3][:, 0:T], ALU.add, ALU.mult)
                    dve.drain()
                    tt(tile(xy, i, T), y, g, ALU.mult).then_inc(conv_done, 1)
                    if phase in CHUNK0:
                        mod_columns(phase, i, 1)
                loop(dve, 0, N_CONV, body)
                phase_done(phase)

            def heads(c, l):
                T, phase, h0 = TOK[c], c + "head", 8 * PASS[c]
                QT = T // P
                NK = T + (CTX if c != "c" else 0)
                mods_per = {a: n for a, _, n in MODS}.get(phase, 0)
                S3 = S[:, :].rearrange("p (m k) -> p m k", m=2)

                def step(i, proj=True, attn=True):
                    for p in range(4):
                        n = At(N0[c] - QT + p, QT, i)
                        if proj:
                            lo(j_at(phase, i, p) + 1)
                        if attn and p < QT:
                            dve.wait_ge(s_ready, shown(s_ready, n + 1))
                            nc.vector.tensor_reduce(small[:, 0:2], S3[:, :, 0:NK], AX_X, ALU.max,
                                                    negate=True).then_inc(nb_ready, 1)
                        if proj and mods_per == 2:
                            mod_tiles(phase, i, p // 2, (0, 1) if p % 2 == 0 else (2, 3))
                            if p == 3:
                                mod_columns(phase, i, 0)
                        if proj and mods_per == 1:
                            mod_tiles(phase, i, 0, (p,))
                        if attn and p < QT:
                            dve.wait_ge(exp_done, shown(exp_done, n + 1))
                            nc.vector.reciprocal(small[:, 4:6], small[:, 2:4])
                            dve.drain()
                            ts(small[:, 6:7], small[:, 5:6], lam[:, l:l + 1], None, ALU.mult)
                            dve.drain()
                            ts(maps[1][:, 0:NK], maps[1][:, 0:NK], small[:, 6:7], None, ALU.mult)
                            dve.drain()
                            stt(maps[0][:, 0:NK], maps[0][:, 0:NK], small[:, 4:5], maps[1][:, 0:NK],
                                ALU.mult, ALU.add).then_inc(a_ready, 1)
                    if proj:
                        dve.wait_ge(acc_free, shown(acc_free, a_at(phase, i, 1) + 1))
                        if attn:
                            dve.wait_ge(s_ready, shown(s_ready, At(N0[c], QT, i)))
                        if c == "c":
                            if attn:
                                dve.wait_ge(k_st, shown(k_st, At(0, 16, i)))
                            nc.vector.tensor_copy(qb[:, 0:T], ev[0][:, 0:T])
                            nc.vector.tensor_copy(kb[:, 0:T], ev[1][:, 0:T]).then_inc(qk_ready, 1)
                        else:
                            for x, o in ((ev[0], qb), (ev[1], kb)):
                                tt(t2[:], x[:], rope[:, 0:SEQ], ALU.mult)
                                nc.vector.stream_shuffle(t1[:], x[:], SWAP)
                                dve.drain()
                                tt(t1[:], t1[:], rope[:, SEQ:2 * SEQ], ALU.mult)
                                dve.drain()
                                last = tt(o[:, 0:SEQ], t1[:], t2[:], ALU.add)
                                dve.drain()
                            dve.sem_inc(qk_ready, 1)
                        dve.wait_ge(acc_free, shown(acc_free, a_at(phase, i, 3) + 1))
                        stt(tile(xy, i + 4, T), evt[:, 0:T], 1.0, ev[3][:, 0:T], ALU.add, ALU.mult).then_inc(gate_used, 1)
                    if attn:
                        dve.wait_ge(ms_done, shown(ms_done, At(h0, 1, i)))
                        ts(t2[:, 0:T], S[:, 1024:1024 + T], 1.0 / P, EPS, ALU.mult, ALU.add).then_inc(var_ready, 1)
                        dve.wait_ge(sd_done, shown(sd_done, At(h0, 1, i)))
                        nc.vector.reciprocal(t2[:, 0:T], t2[:, 0:T])
                        dve.drain()
                        tt(t1[:, 0:T], pv[:, 0:T], t2[:, 0:T], ALU.mult)
                        dve.drain()
                        y = tile(xy, i + 3, T)
                        stt(y, t1[:, 0:T], vec(f"subln{l}"), y, ALU.mult, ALU.mult).then_inc(y_done, 1)
                    if proj and mods_per:
                        mod_columns(phase, i, mods_per - 1)
                step(0, attn=False)
                loop(dve, 1, N_HEADS, step)
                step(N_HEADS, proj=False)
                if phase == "ahead":
                    one_plus((2, 3))
                if phase == "bhead":
                    one_plus((4,))
                phase_done(phase)

            def pooling(c, l):
                T, phase = TOK[c], c + "pool"
                L = T + 2 * PAD
                box = [work[:, 528 * n:528 * n + L] for n in range(3)]
                d = work[:, 1584:1584 + T]
                nc.vector.memset(box[0][:, 0:PAD], 0.0)
                nc.vector.memset(box[0][:, PAD + T:L], 0.0)
                for g, w in enumerate(WINDOWS):
                    for p in range(2):
                        lo(j_at(phase, g, p) + 1)
                    dve.wait_ge(acc_free, shown(acc_free, a_at(phase, g, 0) + 1))
                    u = box[0][:, PAD:PAD + T]
                    nc.vector.tensor_copy(u, ev[0][:, 0:T])
                    src, n, dst = 0, 1, 1
                    while n < w:
                        dve.drain()
                        m = L - 2 * n + 1
                        tt(box[dst][:, 0:m], box[src][:, 0:m], box[src][:, n:n + m], ALU.add)
                        src, n, dst = dst, 2 * n, (2 if dst == 1 else 1)
                    dve.drain()
                    o = PAD - w // 2
                    s = box[src]
                    stt(d, s[:, o:o + T], 1.0 / w, u, ALU.mult, ALU.subtract)
                    for at, e in ((0, 0), (T - 8, 8)):
                        tt(t1[:, e:e + 8], s[:, o + at:o + at + 8], edge[:, 16 * g + e:16 * g + e + 8], ALU.mult)
                    dve.drain()
                    for at, e in ((0, 0), (T - 8, 8)):
                        last = tt(d[:, at:at + 8], t1[:, e:e + 8], u[:, at:at + 8], ALU.subtract)
                    dve.drain()
                    dve.sem_inc(box_ready, 1)
                    dve.wait_ge(acc_free, shown(acc_free, a_at(phase, g, 1) + 1))
                    stt(t2[:, 0:T], evt[:, 0:T], 1.0, ev[3][:, 0:T], ALU.add, ALU.mult)
                    dve.drain()
                    dve.wait_ge(box_mm, shown(box_mm, 4 * PASS[c] + g + 1))
                    stt(tile(xy, 12 + g, T), pv[:, 0:T], vec(f"pool_s{l}", g), t2[:, 0:T],
                        ALU.mult, ALU.mult).then_inc(pool_done, 1)
                phase_done(phase)

            def project_out(c, phase, alpha):
                T = TOK.get(c, SEQ)
                nc.vector.memset(t1[:, 0:T], 0.0)
                dve.drain()

                def body(i, last=False):
                    for p in range(4):
                        if not (last and p == 3):
                            lo(j_at(phase, i, p) + 1)
                        if phase in CHUNK0:
                            mod_tiles(phase, i, p // 2, (0, 1) if p % 2 == 0 else (2, 3))
                            if p == 3:
                                mod_columns(phase, i, 0)
                        dve.wait_ge(acc_free, shown(acc_free, a_at(phase, i, p) + 1))
                        dve.wait_ge(xin_land[p % 2], shown(xin_land[p % 2], At(R_AT[c] // 2 + p // 2, 2, i).times(16) + 16))
                        r = tile(xy, i * 4 + p, T)
                        stt(r, (qb, kb)[p % 2][:, 0:T], alpha, ev[p][:, 0:T], ALU.mult, ALU.add)
                        dve.drain()
                        tt(t1[:, 0:T], t1[:, 0:T], r, ALU.add).then_inc(r_done, 1)
                    if phase in CHUNK0:
                        mod_columns(phase, i, 1)
                if phase == "out2":
                    loop(dve, 0, 3, body)
                    body(3, last=True)
                else:
                    loop(dve, 0, 4, body)
                dve.drain()
                phase_done(phase)

            def norm(c, T, base, count):
                dve.sem_inc(rsum_ready, 1)
                dve.wait_ge(mean_done, shown(mean_done, LN_NO[c] + 1))
                ts(t2[:, 0:T], pv[:, 0:T], 1.0 / (count * P), None, ALU.mult)
                dve.drain()

                def centre(k):
                    x = tile(xy, k + base, T)
                    tt(x, x, t2[:, 0:T], ALU.subtract).then_inc(d_ready, 1)
                loop(dve, 0, count, centre)
                dve.wait_ge(sq_used, shown(sq_used, LN_AT[c] + count))
                ts(t1[:, 0:T], misc[:, 0:T], 1.0 / (count * P), EPS, ALU.mult, ALU.add).then_inc(ln_var, 1)
                dve.wait_ge(ln_sd, shown(ln_sd, LN_NO[c] + 1))
                nc.vector.reciprocal(t1[:, 0:T], t1[:, 0:T])
                dve.drain()

                def scale(k):
                    x = tile(xy, k + base, T)
                    tt(x, x, t1[:, 0:T], ALU.mult).then_inc(n_ready, 1)
                loop(dve, 0, count, scale)

            nc.vector.memset(ones[:], 1.0)
            grant(dve, lo_done, mod_used, mod_out, conv_done, qk_ready, gate_used, var_ready, y_done, r_done, b_used,
                  u2_ready, ypw_done, pool_done, y2_done, gs_done)
            dve.wait_ge(consts, shown(consts, 160))
            dve.wait_ge(setup_act, shown(setup_act, 1))
            stt(t2[:, 0:48], t1[:, 0:48], 1.0, vec("c0", 0, 48), ALU.add, ALU.mult)
            dve.drain()
            ts(csil[:], t2[:, 0:48], 0.5, None, ALU.mult)
            dve.drain()
            dve.sem_inc(setup_dve, 1)
            pairs = work[:, 0:512].rearrange("p (a s d) -> p a s d", s=2, d=QK)
            t1p = t1[:, 0:256].rearrange("p (a d) -> p a d", d=QK)
            tt(t1p, pairs[:, :, 0, :], pairs[:, :, 1, :], ALU.mult)
            dve.drain()
            nc.vector.tensor_reduce(small[:, 0:4], t1p, AX_X, ALU.add).then_inc(setup_dve, 1)
            dve.wait_ge(setup_act, shown(setup_act, 2))
            for l in range(DEPTH):
                tt(lam[:, l:l + 1], small[:, 5 + 2 * l:6 + 2 * l], small[:, 4 + 2 * l:5 + 2 * l], ALU.subtract)
                s = vec(f"subln{l}")
                ts(s, s, 1.0 - LAM_INIT[l], None, ALU.mult)
            dve.drain()
            for l in range(DEPTH):
                ts(lam[:, l:l + 1], lam[:, l:l + 1], -LAM_INIT[l], None, ALU.add)
            for name in ("cln_g", "cln_b"):
                s = vec(name, 0, 8)
                ts(s, s, 0.5, None, ALU.mult)
            dve.wait_ge(setup_pe, shown(setup_pe, 1))
            tt(work[0:16, 912:1296], work[0:16, 912:1296], misc[0:16, 0:384], ALU.add).then_inc(setup_dve, 1)

            def mod0(i):
                for c in range(2):
                    mod_tiles("mod0", i, c, range(MOD_TILES))
                    mod_columns("mod0", i, c)
            loop(dve, 0, 8, mod0)
            one_plus((0, 1))
            phase_done("setup")
            lo(At(0))
            dve.wait_ge(bias_st, shown(bias_st, 16))
            modulate("c.h", 1, lambda i: tile(xy, i, CTX), CTX)
            for c, l in (("c", 0), ("a", 0), ("b", 1)):
                T = TOK[c]
                if c == "a":
                    dve.wait_ge(x_land, shown(x_land, 16))
                    modulate("a.h", 0, lambda i: tile(xy, i, SEQ), SEQ)
                if c == "b":
                    dve.wait_ge(x_ready, shown(x_ready, 32))
                    modulate("b.h", 2, lambda i: tile(xy, i, SEQ), SEQ)
                    dve.wait_ge(x_st, shown(x_st, 32))
                conv(c, l)
                heads(c, l)
                pooling(c, l)
                split_y(c + ".y", T)
                project_out(c, c + "out", ALPHA1)
                if c == "a":
                    dve.wait_ge(x_land, shown(x_land, 32))
                    modulate("kv1", 3, lambda i: work[:, bass.ds(i * CTX, CTX)], CTX, (evt, ev[3]))

                    def kv1(i):
                        for p in range(2):
                            lo(j_at("kv1", i, p) + 1)
                    loop(dve, 0, N_HEADS, kv1)
                    phase_done("kv1")
                norm(c, T, 0, KT)
            dve.wait_ge(x_ready, shown(x_ready, 48))
            modulate("g.h", 4, lambda i: tile(xy, i, SEQ), SEQ)
            dve.wait_ge(x_st, shown(x_st, 48))
            nc.vector.memset(work[:, 0:TAPS - 1], 0.0)
            dve.drain()

            def glu(c):
                for p in range(2):
                    lo(j_at("glu", c, p) + 1)
                dve.wait_ge(acc_free, shown(acc_free, a_at("glu", c, 1) + 1))
                stt(work[:, TAPS - 1:TAPS - 1 + SEQ], evt[:], 1.0, ev[0][:], ALU.add, ALU.mult).then_inc(conv_done, 1)
                dve.drain()
                u = tile(xy, c + 8, SEQ)
                ts(u, work[:, 0:SEQ], vec("dw", c * TAPS), vec("dw_b", c), ALU.mult, ALU.add)
                for tap in range(1, TAPS):
                    dve.drain()
                    stt(u, work[:, tap:tap + SEQ], vec("dw", c * TAPS + tap), u, ALU.mult, ALU.add)
                dve.drain()
            loop(dve, 0, 8, glu)
            nc.vector.tensor_copy(t1[:], tile(xy, 8, SEQ))
            for c in range(1, 8):
                dve.drain()
                tt(t1[:], t1[:], tile(xy, 8 + c, SEQ), ALU.add)
            dve.drain()
            norm("cln", SEQ, 8, 8)

            def conv_silu(i):
                for s in range(2):
                    dve.wait_ge(th_done, shown(th_done, At(s + 1, 2, i)))
                    u = tile(xy, i * 2 + (8 + s), SEQ)
                    stt(u, ev[s][:], 1.0, u, ALU.add, ALU.mult).then_inc(u2_ready, 1)
            loop(dve, 0, 4, conv_silu)
            phase_done("glu")
            for p in range(4):
                lo(j_at("kv2", 0, p) + 1)
            dve.wait_ge(vt_evac, shown(vt_evac, VT0["kv2"] + 2))
            phase_done("kv2")

            def attn2(i, proj=True, attn=True):
                B = ev[1][:, :].rearrange("p (e k) -> p e k", e=2)
                for p in range(2):
                    if proj:
                        lo(j_at("attn2", i, p) + 1)
                    if attn and p == 0:
                        dve.wait_ge(b_ld, shown(b_ld, At(0, 32, i)))
                        dve.wait_ge(pv2_done, shown(pv2_done, At(-1, 1, i)))
                        for e in range(2):
                            o = 8 + 12 * e
                            dve.wait_ge(s2_ready, shown(s2_ready, At(e - 1, 2, i)))
                            last = tt(s2[e][:, P:256], S[:, 1024 * e + P:1024 * e + 256], B[:, e, P:256], ALU.add)
                            last = tt(s2[e][:, 256:1024].rearrange("p (b k) -> p b k", b=3),
                                      S[:, 1024 * e + 256:1024 * (e + 1)].rearrange("p (b k) -> p b k", b=3),
                                      B[:, e:e + 1, :].broadcast_to([P, 3, 256]), ALU.add)
                            dve.drain()
                            if e == 1:
                                dve.sem_inc(b_used, 1)
                            nc.vector.tensor_reduce(small[:, o:o + 1], s2[e][:, P:256], AX_X, ALU.max)
                            nc.vector.tensor_reduce(small[:, o + 1:o + 4],
                                                    s2[e][:, 256:1024].rearrange("p (b k) -> p b k", b=3), AX_X, ALU.max)
                            dve.drain()
                            ts(small[:, o:o + 4], small[:, o:o + 4], sink[:, bass.ds(i * 2 + (e - 2), 1)], -1.0,
                               ALU.max, ALU.mult).then_inc(m2_ready, 1)
                        for e in range(2):
                            o = 8 + 12 * e
                            dve.wait_ge(e2_done, shown(e2_done, At(e - 1, 2, i)))
                            r = small[:, o + 4:o + 8]
                            tt(r, r, small[:, o + 8:o + 12], ALU.add)
                            dve.drain()
                            nc.vector.reciprocal(r, r)
                            dve.drain()
                            for b in range(4):
                                s = s2[e][:, 256 * b + (P if b == 0 else 0):256 * (b + 1)]
                                last = ts(s, s, small[:, o + 4 + b:o + 5 + b], None, ALU.mult)
                            last.then_inc(p2_ready, 1)
                if proj:
                    dve.wait_ge(acc_free, shown(acc_free, a_at("attn2", i, 1) + 1))
                    stt(tile(xy, i, SEQ), evt[:], 1.0, ev[3][:], ALU.add, ALU.mult).then_inc(gate_used, 1)
                if attn:
                    dve.wait_ge(pv2_done, shown(pv2_done, At(0, 1, i)))
                    y = tile(xy, i - 1, SEQ)
                    tt(y, pv[:, :], y, ALU.mult).then_inc(y2_done, 1)
            attn2(0, attn=False)
            loop(dve, 1, 8, attn2)
            attn2(8, proj=False)
            phase_done("attn2")

            def gconv(i):
                for p in range(2):
                    lo(j_at("gconv", i, p) + 1)
                for p in range(2):
                    dve.wait_ge(acc_free, shown(acc_free, a_at("gconv", i, p) + 1))
                    last = stt(work[:, bass.ds(i * 1024 + 512 * p, SEQ)], ev[2 * p + 1][:], 1.0, ev[2 * p][:],
                               ALU.add, ALU.mult)
                last.then_inc(gs_done, 1)
            loop(dve, 0, 4, gconv)
            phase_done("gconv")
            split_y("pw", SEQ, 8, 8)

            def pw(i):
                for t in range(2):
                    lo(j_at("pw", i, t) + 1)
                    for s in range(2):
                        m = 2 * t + s
                        dve.wait_ge(acc_free, shown(acc_free, a_at("pw", i, m) + 1))
                        tt(tile(xy, i * 4 + (8 + m), SEQ), ev[s][:], work[:, bass.ds(i * 2048 + 512 * m, SEQ)],
                           ALU.mult).then_inc(ypw_done, 1)
            loop(dve, 0, 2, pw)
            phase_done("pw")
            split_y("g.y", SEQ)
            project_out("g", "out2", ALPHA2)
            norm("g", SEQ, 0, KT)


SWAP = [i ^ 16 for i in range(32)]


def rope_tables():
    n = QK // 4
    inv = np.float32(10000.0) ** (-np.arange(n, dtype=np.float32) / np.float32(n))
    t = np.arange(SEQ)
    rows, cols = (t // 64).astype(np.float32), (t % 64).astype(np.float32)
    f = np.arange(P) % QK
    pos = np.where((f < QK // 2)[:, None], rows[None], cols[None])
    ang = (pos * inv[f % n][:, None]).astype(np.float32)
    sign = np.where(f % (QK // 2) < n, -1.0, 1.0)[:, None]
    return np.concatenate([np.cos(ang), np.sin(ang) * sign], axis=1).astype(np.float32)


def edge_table():
    T = 64
    out = np.zeros((4, 16), np.float32)
    for g, w in enumerate(WINDOWS):
        for e in range(16):
            t = e if e < 8 else T - 16 + e
            lo, hi = max(t - w // 2, 0), min(t + w - w // 2, T)
            out[g, e] = np.float32(1) / np.float32(hi - lo)
    return np.ascontiguousarray(np.broadcast_to(out.reshape(1, 64), (P, 64)))


def distance_tables():
    d = np.arange(P)
    x = np.maximum(d, 1).astype(np.float32)
    large = 16 + (np.log(x / np.float32(16)) / np.float32(math.log(8)) * np.float32(16)).astype(np.int32)
    bucket = np.where(d < 16, d, np.minimum(large, 31))
    onehot = np.zeros((32, 384), np.float32)
    bar = np.full((16, 384), NEG, np.float32)
    for c in range(P, 256):
        onehot[bucket[255 - c], c] = 1.0
        bar[:, c] = 0.0
    return onehot, bar


def kernel(x, c, ctx, c_ctx, w_mod, b_mod, w_in, conv_w, lam_q1, lam_k1, lam_q2, lam_k2, subln_g,
           pool_w, pool_scale, w_out, ln_g, ln_b, c_2, w_ada_2, b_ada_2, w_in_2, rel_bias_2, sinks_2,
           conv_w_2, conv_b_2, conv_ln_g_2, conv_ln_b_2, w_pw_2, b_pw_2, w_out_2, ln_g_2, ln_b_2):
    import concourse.bacc as bacc
    from concourse.bass_utils import run_bass_kernel_spmd

    def cols(a):
        return np.asarray(a).reshape(-1, P).T

    def tiles(w):
        w = np.asarray(w)
        k, n = w.shape
        return w.reshape(k // P, P, n // P, P).transpose(2, 1, 0, 3).reshape(n // P, P, k)

    def tokens(a):
        return np.ascontiguousarray(np.asarray(a)[0].T.reshape(KT, P, -1).transpose(1, 0, 2))

    def by_group(t):
        order = [g + 4 * p for g in range(4) for p in (0, 2, 1, 3)]
        order += [16 + h + 8 * p for h in range(8) for p in range(4)]
        order += [48 + g + 4 * p for g in range(4) for p in range(2)]
        return t[order]

    def mod_weight(w):
        w = np.asarray(w)
        return w.reshape(4, 4, P, 24, MC).transpose(3, 0, 2, 1, 4).reshape(24 * 4, P, 4 * MC)

    heads2 = [4 * (2 * pair + e) + g for pair in range(2) for g in range(4) for e in range(2)]
    head_cols = np.concatenate([np.arange(64 * h, 64 * h + 64) for h in heads2])
    w2 = np.asarray(w_in_2)[0]
    q2, k2, v2, g2, ga, gb, gc = np.split(w2, np.cumsum([1024, 256, 256, 1024, 1024, 1024]), axis=1)
    q2, g2, ga, gb, gc = (tiles(a) for a in (q2[:, head_cols], g2[:, head_cols], ga, gb, gc))
    pair = lambda a, b: np.stack([a, b], axis=1).reshape(-1, P, D)
    pw = tiles(np.asarray(w_pw_2)[0]).reshape(4, 2, P, D // 2).transpose(0, 2, 1, 3).reshape(4, P, D)
    wo2 = np.asarray(w_out_2)[0]
    wo2 = np.concatenate([wo2[:1024][head_cols], wo2[1024:]], axis=0)

    w_in, w_out = np.asarray(w_in), np.asarray(w_out)
    conv_w, ln_g, ln_b = np.asarray(conv_w), np.asarray(ln_g), np.asarray(ln_b)
    b_mod, pool_scale, subln_g = np.asarray(b_mod), np.asarray(pool_scale), np.asarray(subln_g)
    lams = [np.asarray(a) for a in (lam_q1, lam_k1, lam_q2, lam_k2)]
    vec = {"b_mod0": cols(b_mod[0]), "b_mod1": cols(b_mod[1]), "b_mod2": cols(b_ada_2),
           "conv_w0": cols(conv_w[0]), "conv_w1": cols(conv_w[1]),
           "subln0": cols(subln_g[0]), "subln1": cols(subln_g[1]),
           "pool_s0": cols(pool_scale[0]), "pool_s1": cols(pool_scale[1]),
           "ln_g0": cols(ln_g[0]), "ln_g1": cols(ln_g[1]), "ln_g2": cols(ln_g_2),
           "ln_b0": cols(ln_b[0]), "ln_b1": cols(ln_b[1]), "ln_b2": cols(ln_b_2),
           "dw": np.asarray(conv_w_2)[0].reshape(TAPS, 8, P).transpose(2, 1, 0).reshape(P, 8 * TAPS),
           "dw_b": cols(conv_b_2), "cln_g": cols(conv_ln_g_2), "cln_b": cols(conv_ln_b_2), "b_pw": cols(b_pw_2),
           "c0": cols(c), "c1": cols(c_ctx), "c2": cols(c_2)}
    onehot, bar = distance_tables()
    arrays = {
        "w0": np.concatenate([by_group(tiles(w_in[0])), tiles(w_out[0])]),
        "w1": np.concatenate([by_group(tiles(w_in[1])), tiles(w_out[1])]),
        "w2": np.concatenate([pair(ga, gb), tiles(k2), tiles(v2), pair(q2, g2), gc, pw, tiles(wo2)]),
        "wm": np.concatenate([mod_weight(w_mod[0]), mod_weight(w_mod[1]), mod_weight(np.asarray(w_ada_2)[0])]),
        "xT": tokens(x), "ctxT": tokens(ctx),
        "vecs": np.concatenate([vec[n] for n, _ in VECS], axis=1),
        "lam": np.stack([lams[2 * a + s][l] for l in range(DEPTH) for a in range(2) for s in range(2)]).reshape(512),
        "sinks": np.asarray(sinks_2)[0][heads2],
        "rel_bias": np.asarray(rel_bias_2)[:, heads2],
        "pool_w": np.asarray(pool_w).transpose(0, 2, 1, 3).reshape(DEPTH, P, 512),
        "ident": np.eye(P, dtype=np.float32), "rope": rope_tables(), "edge": edge_table(),
        "onehot": onehot, "negmask": bar,
    }
    arrays = {f"in_{n}": np.ascontiguousarray(a) for n, a in arrays.items()}
    nc = bacc.Bacc("TRN2", target_bir_lowering=False, num_devices=1)
    aps = {n[3:]: nc.dram_tensor(n, a.shape, F32, kind="ExternalInput").ap() for n, a in arrays.items()}
    out = nc.dram_tensor("out_y", (P, KT, SEQ), F32, kind="ExternalOutput").ap()
    build(nc, aps, out)
    r = run_bass_kernel_spmd(nc, [arrays], core_ids=[0])
    y = r.results[0]["out_y"]
    return np.ascontiguousarray(y.transpose(1, 0, 2).reshape(D, SEQ).T)[None]
```

```python
import math
from contextlib import ExitStack

import numpy as np

import concourse.bass as bass
from concourse import mybir

F32 = mybir.dt.float32
F32R = mybir.dt.float32r
ALU = mybir.AluOpType
ACT = mybir.ActivationFunctionType
AX_X = mybir.AxisListType.X

P = 128
D = 2048
KT = D // P
SEQ, CTX = 512, 256
N_HEADS, QK = 8, 64
N_CONV, N_POOL = 4, 4
WINDOWS = (2, 4, 8, 16)
PAD = max(WINDOWS) // 2
EPS = 1e-5
DEPTH = 2
ALPHA1 = (2.0 * DEPTH) ** 0.25
ALPHA2 = 2.0 ** 0.25
TAPS = 31
BLOCK = 128
NEG = -3.0e38
MC = 512
MOD_KT = 2
MOD_TILES = KT // MOD_KT
MOD_COLS = MC // P
LAM_INIT = tuple(0.8 - 0.6 * math.exp(-0.3 * l) for l in range(DEPTH))

VECS = [("b_mod0", 48), ("b_mod1", 48), ("b_mod2", 48), ("conv_w0", 12), ("conv_w1", 12),
        ("subln0", 1), ("subln1", 1), ("pool_s0", 4), ("pool_s1", 4),
        ("ln_g0", 16), ("ln_g1", 16), ("ln_g2", 16), ("ln_b0", 16), ("ln_b1", 16), ("ln_b2", 16),
        ("dw", 8 * TAPS), ("dw_b", 8), ("cln_g", 8), ("cln_b", 8), ("b_pw", 8),
        ("c0", 16), ("c1", 16), ("c2", 16)]
VEC_AT = {}
_at = 0
for _n, _w in VECS:
    VEC_AT[_n] = _at
    _at += _w
NVEC = _at

STREAM = [("cconv", 4, 4), ("chead", 8, 4), ("cpool", 4, 2), ("cout", 4, 4),
          ("aconv", 4, 4), ("ahead", 8, 4), ("apool", 4, 2), ("aout", 4, 4),
          ("kv1", 8, 2),
          ("bconv", 4, 4), ("bhead", 8, 4), ("bpool", 4, 2), ("bout", 4, 4),
          ("glu", 4, 6), ("kv2", 1, 4), ("attn2", 8, 2), ("pw", 2, 2), ("out2", 4, 4)]
TILE0 = {}
_at = 0
for _n, _i, _t in STREAM:
    TILE0[_n] = _at
    _at += _i * _t
N_TILES = _at
MODS = [("mod0", 4, 1), ("aconv", 4, 1), ("ahead", 4, 1), ("aout", 4, 1), ("bconv", 4, 1), ("bhead", 4, 1),
        ("bout", 4, 1)]
MOD0_CHUNKS = 8
CHUNK0 = {}
_at = 0
for _n, _i, _t in MODS:
    CHUNK0[_n] = _at
    _at += _i * _t
MOD_OF = {"mod0": ((0, 1), 32), "aconv": ((2, 3), 0), "ahead": ((2, 3), 16), "aout": ((2,), 32),
          "bconv": ((4,), 0), "bhead": ((4,), 16), "bout": ((4,), 32)}
MOD_VEC = (0, 1, 0, 1, 2)
MOD_LAYER = (0, 0, 1, 1, 2)


class At:

    def __init__(self, c, k=0, i=0):
        if isinstance(i, int):
            c, k, i = c + k * i, 0, 0
        self.c, self.k, self.i = c, k, i

    def __add__(self, n):
        return At(self.c + n, self.k, self.i)

    def __sub__(self, n):
        return self + -n

    @property
    def odd(self):
        assert self.k % 2 == 0
        return self.c % 2

    @property
    def half(self):
        assert self.k % 2 == 0
        return At(self.c // 2, self.k // 2, self.i)

    def times(self, n):
        return At(self.c * n, self.k * n, self.i)

    @property
    def val(self):
        return self.i * self.k + self.c if self.k else self.c


def build(nc, A, out):
    with ExitStack() as ctx:
        def sb(name, cols, dt=F32, rows=P):
            return ctx.enter_context(nc.sbuf_tensor(name, [rows, cols], dt))

        def psum(name, cols):
            return ctx.enter_context(nc.psum_tensor(name, [P, cols], F32))

        credits = {}

        def sem(name, credit=0):
            s = ctx.enter_context(nc.semaphore(name))
            credits[id(s)] = credit
            return s

        def dram(name, shape):
            return nc.dram_tensor(name, shape, F32, kind="Internal").ap()

        raw = sb("raw", 2 * D)
        w_hi = sb("w_hi", 2 * D, F32R)
        w_lo = sb("w_lo", 2 * D, F32R)
        h_hi = sb("h_hi", KT * SEQ, F32R)
        h_lo = sb("h_lo", KT * SEQ, F32R)
        xy = sb("xy", KT * SEQ)
        gates = sb("gates", 8 * SEQ)
        mraw = gates[:, 0:2 * MOD_KT * MC]
        macc = gates[:, 2048:2048 + 2 * MC]
        rope = gates[:, 3072:3072 + 2 * SEQ]
        ev = [sb(f"ev{n}", SEQ) for n in range(4)]
        evt = sb("evt", SEQ)
        work = sb("work", 4608)
        qb = sb("qb", SEQ)
        kb = sb("kb", SEQ + CTX)
        vtok = sb("vtok", 1024)
        t1 = sb("t1", SEQ)
        t2 = sb("t2", SEQ)
        vecs = sb("vecs", NVEC)
        modc = sb("modc", 5 * 48)
        csil = sb("csil", 48)
        ident = sb("ident", P)
        ones = sb("ones", P)
        edge = sb("edge", 4 * 16)
        lam = sb("lam", 2 * 8)
        sink = sb("sink", 16)
        small = sb("small", 32)

        acc = [psum(f"acc{n}", 512) for n in range(2)]
        S = psum("S", 2048)
        pv = psum("pv", 512)
        misc = psum("misc", 512)
        gate0 = (mraw[:, 0:MOD_KT * MC], mraw[:, MOD_KT * MC:], rope, vtok[:, :])
        whole = (evt, ev[3])
        mod_ps = misc[:, 0:2 * MOD_COLS]

        xy3 = xy[:, :].rearrange("p (k t) -> p k t", t=SEQ)
        maps = [work[:, (SEQ + CTX) * m:(SEQ + CTX) * (m + 1)] for m in range(2)]
        a_t = work[:, 1536:1536 + 6 * SEQ]
        osq = a_t[:, 0:SEQ]
        POOLW = 2096
        s2 = [work[:, 1024 * e:1024 * (e + 1)] for e in range(2)]
        k2 = work[:, 2048:3072]

        k_ctx = dram("k_ctx", (DEPTH, N_HEADS, P, CTX))
        v_ctx = dram("v_ctx", (DEPTH, N_HEADS, P, CTX))
        c1_d = dram("c1_d", (P, KT, CTX))
        x1_d = dram("x1_d", (P, KT, SEQ))
        x2_d = dram("x2_d", (P, KT, SEQ))
        bias_d = dram("bias_d", (16 * P * 384 + 384,))

        m0_landed = [sem(f"m0_landed{n}") for n in range(4)]
        m0_used = sem("m0_used", 4)
        m0_row = sem("m0_row", 2)
        m0_cols = sem("m0_cols", 2)
        raw_landed = [sem(f"raw_landed{n}") for n in range(2)]
        hi_done = sem("hi_done")
        lo_done = sem("lo_done", 2)
        tile_done = sem("tile_done", 2)
        acc_free = sem("acc_free", 2)
        mraw_landed = [sem(f"mraw_landed{n}") for n in range(2)]
        gate0_landed = [sem(f"gate0_landed{n}") for n in range(4)]
        mod_used = sem("mod_used", 4)
        macc_ready = sem("macc_ready")
        mod_out = sem("mod_out", 1)
        mod_red = sem("mod_red")
        pool_step = sem("pool_step")
        vecs_land = sem("vecs_land")
        consts = sem("consts")
        rope_land = sem("rope_land")
        late_consts = sem("late_consts")
        setup_act = sem("setup_act")
        setup_dve = sem("setup_dve")
        setup_pe = sem("setup_pe")
        bias_st = sem("bias_st")
        x_land = sem("x_land")
        hhi_done = sem("hhi_done")
        hlo_done = sem("hlo_done", 2)
        dve_phase = sem("dve_phase")
        conv_done = sem("conv_done", 1)
        box_ready = sem("box_ready")
        box_mm = sem("box_mm")
        pool_w_land = sem("pool_w_land")
        qk_ready = sem("qk_ready", 1)
        gate_used = sem("gate_used", 1)
        s_ready = sem("s_ready", 4)
        nb_ready = sem("nb_ready")
        exp_done = sem("exp_done", 4)
        a_ready = sem("a_ready")
        t_done = sem("t_done", 1)
        at_evac = sem("at_evac", 4)
        pv_done = sem("pv_done", 1)
        osq_done = sem("osq_done")
        ms_done = sem("ms_done")
        var_ready = sem("var_ready", 1)
        sd_done = sem("sd_done")
        y_done = sem("y_done", 1)
        vt_done = sem("vt_done", 1)
        vt_evac = sem("vt_evac", 1)
        k_st = sem("k_st")
        v_st = sem("v_st")
        k_ld = sem("k_ld")
        v_ld = sem("v_ld")
        xin_land = [sem(f"xin_land{n}") for n in range(2)]
        r_done = sem("r_done", 4)
        mean_done = sem("mean_done")
        d_ready = sem("d_ready")
        sq_ready = sem("sq_ready")
        sq_used = sem("sq_used", 4)
        sq_added = sem("sq_added", 1)
        sqsum_ready = sem("sqsum_ready")
        ln_var = sem("ln_var")
        ln_sd = sem("ln_sd")
        n_ready = sem("n_ready")
        x_ready = sem("x_ready")
        x_st = sem("x_st")
        b_ld = sem("b_ld")
        b_used = sem("b_used", 1)
        s2_ready = sem("s2_ready")
        m2_ready = sem("m2_ready")
        e2_done = sem("e2_done")
        p2_ready = sem("p2_ready")
        t2_done = sem("t2_done")
        t2_evac = sem("t2_evac", 2)
        pv2_done = sem("pv2_done", 1)
        u2_ready = sem("u2_ready", 2)
        th_done = sem("th_done")
        pw_done = sem("pw_done")
        ypw_done = sem("ypw_done", 2)
        pool_done = sem("pool_done", 1)
        y2_done = sem("y2_done", 1)
        gs_done = sem("gs_done", 1)
        rsum_ready = sem("rsum_ready")

        def shown(s, n):
            n = (n if isinstance(n, At) else At(n)) + credits[id(s)]
            assert n.c > 0 or n.k, "a wait for nothing"
            return n.val

        def grant(eng, *sems):
            for s in sems:
                eng.sem_inc(s, credits[id(s)])

        def vec(name, c=0, n=1):
            a = VEC_AT[name]
            return vecs[:, bass.ds(c + a, n)]

        def mod(which, what, m):
            return modc[:, bass.ds(m + (48 * which + 16 * what), 1)]

        def by_set(which):
            return (lambda k: mod(which, 1, k)), (lambda k: mod(which, 0, k))

        def ctx_tile(k):
            return work[:, bass.ds(k * CTX, CTX)]

        def late_x(k):
            return work[:, bass.ds(k * SEQ + -KT // 2 * SEQ, SEQ)]

        def tile(t, k, T):
            return t[:, bass.ds(k * SEQ, T)]

        def part(c, k, T=SEQ):
            return xy[:, bass.ds(k * CTX + KT * CTX, CTX)] if c == "c" else tile(xy, k, T)

        def norm_buffers(c):
            if c == "c":
                return kb[:, 0:CTX], qb[:, 0:CTX], pv, [vtok[:, CTX * n:CTX * (n + 1)] for n in range(4)]
            return t2, t1, (pv if c == "a" else misc), \
                {"a": (ev[0], ev[1], ev[3], evt), "cln": (ev[0], ev[2])}.get(c, ev)

        def loop(eng, first, last, body):
            with eng.Fori(first, last) as i:
                body(i)

        PASS = {"c": 0, "a": 1, "b": 2}
        TOK = {"c": CTX, "a": SEQ, "b": SEQ}
        N0 = {"c": 0, "a": 2 * N_HEADS, "b": 2 * N_HEADS + 4 * N_HEADS}
        H_AT = {"c.h": 0, "c.y": 16, "a.h": 32, "a.y": 48, "kv1": 64, "b.h": 80, "b.y": 96, "g.h": 112,
                "pw": 128, "g.y": 136}
        DVE_PHASES = ["setup", "cconv", "chead", "cpool", "cout", "aconv", "ahead", "apool", "aout", "kv1",
                      "bconv", "bhead", "bpool", "bout", "kv2", "attn2", "pw", "out2"]
        LN_AT = {"c": 0, "a": 16, "b": 32, "cln": 48, "g": 56}
        SQ_AT = {"c": 0, "a": 1, "b": 2, "cln": 18, "g": 26}
        LN_NO = {"c": 0, "a": 1, "b": 2, "cln": 3, "g": 4}
        VT0 = {"c": 0, "a": 8, "kv1": 16, "b": 24, "kv2": 32}
        CONV0 = {"c": 0, "a": 4, "b": 8, "glu": 12}
        R_AT = {"c": 0, "a": 16, "b": 32, "g": 48}

        def after(phase):
            return DVE_PHASES.index(phase) + 1

        def j_at(phase, i, p=0):
            t = {n: t for n, _, t in STREAM}[phase]
            return At(TILE0[phase] + p, t, i)

        def a_at(phase, i, p=0):
            if phase == "pw":
                return At(TILE0["pw"] + p, 4, i)
            return j_at(phase, i, p) + (4 if phase == "out2" else 0)

        def chunk_at(phase, i, p=0):
            return At(CHUNK0[phase] + p, {n: t for n, _, t in MODS}[phase], i)

        block = ctx.enter_context(nc.Block())

        @block.sync
        def _(sp):
            def load(j, src):
                sp.wait_ge(lo_done, shown(lo_done, j - 1))
                sp.dma_start(raw[:, j.odd * D:(j.odd + 1) * D], src).then_inc(raw_landed[j.odd], 16)

            def stream(phase, w, t0):
                n_iter, tiles = {n: (i, t) for n, i, t in STREAM}[phase]

                def body(i):
                    for p in range(tiles):
                        load(j_at(phase, i, p), w[bass.ds(i * tiles + (t0 + p), 1)])
                if n_iter == 1:
                    body(0)
                else:
                    loop(sp, 0, n_iter, body)

            def mod0(i):
                for s in range(4):
                    sp.wait_ge(m0_used, shown(m0_used, At(s - 3, 4, i)))
                    sp.dma_start(xy[:, s * D:(s + 1) * D].rearrange("p (t n) -> p t n", t=2),
                                 A["wm"][bass.ds(i * 8 + 2 * s, 2)].rearrange("t p n -> p t n")).then_inc(m0_landed[s], 16)
            loop(sp, 0, MOD0_CHUNKS, mod0)
            w0, w1, w2 = A["w0"], A["w1"], A["w2"]
            for c in "ca":
                for phase, t0 in (("conv", 0), ("head", 16), ("pool", 48), ("out", 56)):
                    stream(c + phase, w0, t0)

            def kv(i):
                for p, t in ((0, 18), (1, 17)):
                    load(j_at("kv1", i, p), w1[bass.ds(i * 4 + t, 1)])
            loop(sp, 0, N_HEADS, kv)
            for phase, t0 in (("conv", 0), ("head", 16), ("pool", 48), ("out", 56)):
                stream("b" + phase, w1, t0)
            at = 0
            for phase in ("glu", "kv2", "attn2", "pw", "out2"):
                stream(phase, w2, at)
                n, i, t = [s for s in STREAM if s[0] == phase][0]
                at += i * t


        @block.gpsimd
        def _(pool):
            def mods(phase, i, tiles=range(MOD_TILES), per=MOD_TILES):
                sets, col = MOD_OF[phase]
                first = (3 * D // MC * MOD_LAYER[sets[0]] + col // MOD_COLS) * MOD_TILES
                for t in tiles:
                    m = At(CHUNK0[phase] * MOD_TILES + t, per, i)
                    pool.wait_ge(mod_used, shown(mod_used, m - 1))
                    pool.sem_inc(pool_step, 1)
                    pool.dma_start(mraw[:, m.odd * MOD_KT * MC:(m.odd + 1) * MOD_KT * MC],
                                   A["wm"][bass.ds(i * per + (first + t), 1)]).then_inc(mraw_landed[m.odd], 16)

            def head_step(c):
                def step(i, attn=True):
                    if c + "head" in CHUNK0:
                        mods(c + "head", i, range(MOD_TILES // 2), MOD_TILES // 2)
                    if c == "c":
                        pool.wait_ge(qk_ready, shown(qk_ready, At(1, 1, i)))
                        pool.sem_inc(pool_step, 1)
                        pool.dma_start(k_ctx[0][bass.ds(i, 1)], kb[:, 0:CTX]).then_inc(k_st, 16)
                        pool.wait_ge(vt_evac, shown(vt_evac, At(1, 1, i)))
                        pool.sem_inc(pool_step, 1)
                        pool.dma_start(v_ctx[0][bass.ds(i, 1)], vtok[:, 0:CTX]).then_inc(v_st, 16)
                        return
                    l = PASS[c] - 1
                    if attn:
                        pool.wait_ge(s_ready, shown(s_ready, At(N0[c], 4, i)))
                        pool.sem_inc(pool_step, 1)
                    pool.dma_start(kb[:, SEQ:SEQ + CTX], k_ctx[l][bass.ds(i, 1)]).then_inc(k_ld, 16)
                    if attn:
                        pool.wait_ge(pv_done, shown(pv_done, At(8 * PASS[c], 1, i)))
                        pool.sem_inc(pool_step, 1)
                    pool.dma_start(vtok[:, SEQ:SEQ + CTX], v_ctx[l][bass.ds(i, 1)]).then_inc(v_ld, 16)
                step(0, attn=False)
                loop(pool, 1, N_HEADS, step)

            def pool_weights(l, phase):
                pool.wait_ge(dve_phase, shown(dve_phase, after(phase)))
                pool.dma_start(work[:, POOLW:POOLW + 512], A["pool_w"][l]).then_inc(pool_w_land, 16)

            def residual(c, phase, x):
                T = TOK.get(c, SEQ)

                def body(i):
                    for p in range(4):
                        if phase in CHUNK0:
                            mods(phase, i, range(2 * p, 2 * p + 2))
                        pool.wait_ge(r_done, shown(r_done, At(R_AT[c] + p - 1, 4, i)))
                        pool.sem_inc(pool_step, 1)
                        pool.dma_start((qb, kb)[p % 2][:, 0:T],
                                       x[:, bass.ds(i * 4 + p, 1), :]).then_inc(xin_land[p % 2], 16)
                loop(pool, 0, 4, body)

            def store(c, dst, count):
                pool.wait_ge(x_ready, shown(x_ready, count))
                pool.dma_start(dst, xy3 if c != "c" else xy[:, KT * CTX:].rearrange("p (k t) -> p k t", t=CTX))\
                    .then_inc(x_st, 16)

            pool.dma_start(vecs[:], A["vecs"]).then_inc(vecs_land, 16)
            for dst, src in ((ident[:], A["ident"]), (ev[2][:], A["lam"].partition_broadcast(P)),
                             (sink[:], A["sinks"].partition_broadcast(P)),
                             (ev[3][0:32, 0:16], A["rel_bias"]), (ev[3][0:32, 16:400], A["onehot"]),
                             (evt[0:16, 0:384], A["negmask"])):
                pool.dma_start(dst, src).then_inc(consts, 16)

            def gates0(i):
                first = (2 * D // MC) * MOD_TILES
                for t in range(MOD_TILES):
                    pool.wait_ge(mod_used, shown(mod_used, At(t - 3, MOD_TILES, i)))
                    pool.sem_inc(pool_step, 1)
                    pool.dma_start(gate0[t % 4], A["wm"][bass.ds(i * MOD_TILES + (first + t), 1)])\
                        .then_inc(gate0_landed[t % 4], 16)
            loop(pool, 0, 4, gates0)
            for dst, src in ((edge[:], A["edge"]),
                             (work[:, 0:KT * CTX].rearrange("p (k t) -> p k t", t=CTX), A["ctxT"])):
                pool.dma_start(dst, src).then_inc(late_consts, 16)
            pool.wait_ge(mod_used, shown(mod_used, 4 * MOD_TILES))
            pool.dma_start(rope, A["rope"]).then_inc(rope_land, 16)
            pool.wait_ge(setup_dve, shown(setup_dve, 3))
            pool.dma_start(bias_d[0:16 * P * 384].rearrange("(h q n) -> h q n", q=P, n=384),
                           evt[0:16, 0:384].unsqueeze(1).broadcast_to([16, P, 384])).then_inc(bias_st, 16)
            head_step("c")
            pool_weights(0, "chead")
            pool.wait_ge(dve_phase, shown(dve_phase, after("cpool")))
            pool.dma_start(xy3[:, 0:KT // 2], A["xT"][:, 0:KT // 2]).then_inc(x_land, 16)
            pool.dma_start(work[:, 0:KT // 2 * SEQ].rearrange("p (k t) -> p k t", t=SEQ),
                           A["xT"][:, KT // 2:]).then_inc(x_land, 16)
            residual("c", "cout", A["ctxT"])
            pool.wait_ge(k_st, shown(k_st, 16 * N_HEADS))
            pool.wait_ge(v_st, shown(v_st, 16 * N_HEADS))
            loop(pool, 0, 4, lambda i: mods("aconv", i))
            store("c", c1_d, 16)
            pool.wait_ge(dve_phase, shown(dve_phase, after("aconv")))
            head_step("a")
            pool_weights(0, "ahead")
            pool.wait_ge(dve_phase, shown(dve_phase, after("apool")))
            pool.wait_ge(x_st, shown(x_st, 16))
            pool.dma_start(work[:, 0:KT * CTX].rearrange("p (k t) -> p k t", t=CTX), c1_d).then_inc(x_land, 16)
            residual("a", "aout", A["xT"])

            def kv1_store(i):
                pool.wait_ge(acc_free, shown(acc_free, a_at("kv1", i, 1) + 1))
                pool.sem_inc(pool_step, 1)
                pool.dma_start(k_ctx[1][bass.ds(i, 1)], kb[:, 0:CTX]).then_inc(k_st, 16)
                pool.wait_ge(vt_evac, shown(vt_evac, At(VT0["kv1"] + 1, 1, i)))
                pool.sem_inc(pool_step, 1)
                pool.dma_start(v_ctx[1][bass.ds(i, 1)], vtok[:, 0:CTX]).then_inc(v_st, 16)
            loop(pool, 0, N_HEADS, kv1_store)
            store("a", x1_d, 32)
            loop(pool, 0, 4, lambda i: mods("bconv", i))
            pool.wait_ge(k_st, shown(k_st, 2 * 16 * N_HEADS))
            pool.wait_ge(v_st, shown(v_st, 2 * 16 * N_HEADS))
            pool.wait_ge(x_st, shown(x_st, 32))
            pool.wait_ge(dve_phase, shown(dve_phase, after("bconv")))
            head_step("b")
            pool_weights(1, "bhead")
            pool.wait_ge(dve_phase, shown(dve_phase, after("bpool")))
            residual("b", "bout", x1_d)
            store("b", x2_d, 48)
            pool.wait_ge(bias_st, shown(bias_st, 16))
            pool.wait_ge(dve_phase, shown(dve_phase, after("kv2")))

            def biases(i):
                pool.wait_ge(b_used, shown(b_used, At(0, 1, i)))
                pool.sem_inc(pool_step, 1)
                for e in range(2):
                    rows = bass.AP(bias_d.tensor, i * (2 * P * 384) + (e * P * 384 + BLOCK - 1), [[383, P], [1, 256]])
                    pool.dma_start(ev[1][:, 256 * e:256 * e + 256], rows).then_inc(b_ld, 16)
            loop(pool, 0, 8, biases)
            pool.wait_ge(x_st, shown(x_st, 48))
            pool.wait_ge(dve_phase, shown(dve_phase, after("pw")))
            residual("g", "out2", x2_d)
            for q in range(4):
                pool.wait_ge(x_ready, shown(x_ready, 48 + 4 * (q + 1)))
                pool.dma_start(out[:, 4 * q:4 * (q + 1)], xy3[:, 4 * q:4 * (q + 1)]).then_inc(x_st, 16)
            pool.wait_ge(x_st, shown(x_st, 48 + 64))

        @block.scalar
        def _(act):
            def f(out, in_, func=ACT.Copy, **kw):
                return nc.scalar.activation(out, in_, func, **kw)

            def hi(j):
                act.wait_ge(raw_landed[j.odd], shown(raw_landed[j.odd], j.half.times(16) + 16))
                act.wait_ge(tile_done, shown(tile_done, j - 1))
                f(w_hi[:, j.odd * D:(j.odd + 1) * D], raw[:, j.odd * D:(j.odd + 1) * D]).then_inc(hi_done, 1)

            def modulate(c, src, T, scale, bias, first=0, last=KT, normed=None):
                def body(i):
                    for s in range(2):
                        k = i * 2 + s
                        if normed is not None:
                            act.wait_ge(n_ready, shown(n_ready, At(normed + s + 1, 2, i)))
                        if s == 0 or normed is not None:
                            act.wait_ge(hlo_done, shown(hlo_done, At(H_AT[c] + s - 1, 2, i)))
                            f(whole[s][:, 0:T], src(k), ACT.Identity, scale=scale(k), bias=bias(k))
                        f(tile(h_hi, k, T), src(k), ACT.Identity, scale=scale(k), bias=bias(k)).then_inc(hhi_done, 1)
                loop(act, first // 2, last // 2, body)

            def split_y(c, T, first=0, last=KT, base=0):
                def body(i):
                    for s in range(4):
                        f(tile(h_hi, i * 4 + s, T), part(c, i * 4 + (base + s), T)).then_inc(hhi_done, 1)
                loop(act, first // 4, last // 4, body)

            def half_and_tanh(x, half, th):
                f(half, x, ACT.Copy, scale=0.5)
                return f(th, x, ACT.Tanh, scale=0.5)

            def conv(c):
                T, phase = TOK[c], c + "conv"

                def body(g, ctx_norm=None):
                    for p in range(4):
                        j, a = j_at(phase, g, p), a_at(phase, g, p)
                        hi(j + 1)
                        x = acc[a.odd][:, 0:T]
                        if p == 0:
                            act.wait_ge(conv_done, shown(conv_done, At(CONV0[c], 1, g)))
                        act.wait_ge(tile_done, shown(tile_done, j + 1))
                        if p < 3:
                            f(ev[p][:, 0:T], x).then_inc(acc_free, 1)
                        else:
                            half_and_tanh(x, ev[3][:, 0:T], evt[:, 0:T]).then_inc(acc_free, 1)
                        if ctx_norm == 0:
                            squares_to_add("c", CTX, p)
                        if ctx_norm == 1 and p == 1:
                            deviation("c", CTX)
                        if ctx_norm == 1 and p == 3:
                            norm_affine("c", CTX, 0)
                if c == "a":
                    act.wait_ge(v_st, shown(v_st, 16 * N_HEADS))
                    body(0, ctx_norm=0)
                    body(1, ctx_norm=1)
                    loop(act, 2, N_CONV, body)
                else:
                    loop(act, 0, N_CONV, body)

            def heads(c):
                T, phase, h0 = TOK[c], c + "head", 8 * PASS[c]
                QT = T // P
                NK = T + (CTX if c != "c" else 0)

                def root(i):
                    act.wait_ge(var_ready, shown(var_ready, At(h0 - 1, 1, i)))
                    f(t2[:, 0:T], t2[:, 0:T], ACT.Sqrt).then_inc(sd_done, 1)

                def step(i, proj=True, attn=True, norm=True):
                    for p in range(4):
                        j, a = j_at(phase, i, p), a_at(phase, i, p)
                        n = At(N0[c] - QT + p, QT, i)
                        hi(j + 1 if proj else j_at(c + "pool", 0, p + 1))
                        if attn and p < QT:
                            act.wait_ge(nb_ready, shown(nb_ready, n + 1))
                            act.wait_ge(t_done, shown(t_done, n))
                            for m in range(2):
                                e = f(maps[m][:, 0:NK], S[:, 1024 * m:1024 * m + NK], ACT.Exp,
                                      bias=small[:, m:m + 1], accum_out=small[:, 2 + m:3 + m])
                            e.then_inc(exp_done, 1)
                        if norm and p == 0:
                            root(i)
                        if proj:
                            x = acc[a.odd][:, 0:T]
                            if p == 0:
                                act.wait_ge(qk_ready, shown(qk_ready, At(h0, 1, i)))
                            if p == 2:
                                act.wait_ge(vt_done, shown(vt_done, At(VT0[c], 1, i)))
                            if p == 3:
                                act.wait_ge(gate_used, shown(gate_used, At(h0, 1, i)))
                            act.wait_ge(tile_done, shown(tile_done, j + 1))
                            if p == 0:
                                f(ev[0][:, 0:T], x, scale=QK ** -0.5).then_inc(acc_free, 1)
                            elif p < 3:
                                f(ev[p][:, 0:T], x).then_inc(acc_free, 1)
                            else:
                                half_and_tanh(x, ev[3][:, 0:T], evt[:, 0:T]).then_inc(acc_free, 1)
                        else:
                            pool_tile(c, p)
                        if attn and p < QT:
                            act.wait_ge(t_done, shown(t_done, n + 1))
                            if p == 0:
                                act.wait_ge(pv_done, shown(pv_done, At(h0 - 1, 1, i)))
                            f(a_t[:, 0:NK // P * T].rearrange("p (k t) -> p k t", t=T)[:, :, P * p:P * (p + 1)],
                              S[:, 0:NK].rearrange("p (k q) -> p k q", q=P)).then_inc(at_evac, 1)
                    if attn:
                        act.wait_ge(pv_done, shown(pv_done, At(h0, 1, i)))
                        f(osq[:, 0:T], pv[:, 0:T], ACT.Square).then_inc(osq_done, 1)
                    if proj:
                        act.wait_ge(vt_done, shown(vt_done, At(VT0[c] + 1, 1, i)))
                        if c == "c" and attn:
                            act.wait_ge(v_st, shown(v_st, At(0, 16, i)))
                        f(vtok[:, 0:T], misc[:, 0:T]).then_inc(vt_evac, 1)
                act.wait_ge(dve_phase, shown(dve_phase, after(c + "conv")))
                step(0, attn=False, norm=False)
                step(1, norm=False)
                loop(act, 2, N_HEADS, step)
                act.wait_ge(qk_ready, shown(qk_ready, h0 + N_HEADS))
                act.wait_ge(vt_done, shown(vt_done, VT0[c] + N_HEADS))
                act.wait_ge(gate_used, shown(gate_used, h0 + N_HEADS))
                step(N_HEADS, proj=False)
                root(N_HEADS + 1)

            def pool_tile(c, t):
                phase, T, g = c + "pool", TOK[c], t // 2
                j, a = j_at(phase, 0, t), a_at(phase, 0, t)
                if g >= 2:
                    act.wait_ge(pool_done, shown(pool_done, 4 * PASS[c] + g - 1))
                act.wait_ge(tile_done, shown(tile_done, j + 1))
                u, half, th = ((ev[0], ev[3], evt), (ev[1], ev[2], t1))[g % 2]
                x = acc[a.odd][:, 0:T]
                if t % 2 == 0:
                    f(u[:, 0:T], x).then_inc(acc_free, 1)
                else:
                    half_and_tanh(x, half[:, 0:T], th[:, 0:T]).then_inc(acc_free, 1)

            def pooling(c):

                for t in range(4, 8):
                    hi(j_at(c + "pool", 0, t) + 1)
                    pool_tile(c, t)

            def project_out(c, phase, which):
                T = TOK.get(c, SEQ)

                def body(i, last=False):
                    for p in range(4):
                        j, a = j_at(phase, i, p), a_at(phase, i, p)
                        if not (last and p == 3):
                            hi(j + 1)
                        act.wait_ge(r_done, shown(r_done, At(R_AT[c] + p - 3, 4, i)))
                        act.wait_ge(tile_done, shown(tile_done, j + 1))
                        f(ev[p][:, 0:T], acc[a.odd][:, 0:T], scale=mod(which, 2, i * 4 + p)).then_inc(acc_free, 1)
                if phase == "out2":
                    loop(act, 0, 3, body)
                    body(3, last=True)
                else:
                    loop(act, 0, 4, body)

            def squares_to_add(c, T, g):
                to = norm_buffers(c)[3]
                at = LN_AT[c]
                act.wait_ge(sq_added, shown(sq_added, At(at, 4, g)))
                for n in range(4):
                    act.wait_ge(d_ready, shown(d_ready, At(at + n + 1, 4, g)))
                    f(to[n][:, 0:T], part(c, g * 4 + n, T), ACT.Square).then_inc(sq_ready, 1)

            def squares(c, T, base, count):
                to = norm_buffers(c)[3]
                N = len(to)

                def body(i):
                    for n in range(N):
                        act.wait_ge(d_ready, shown(d_ready, At(LN_AT[c] + n + 1, N, i)))
                        act.wait_ge(sq_used, shown(sq_used, At(SQ_AT[c] + n + 1 - N, N, i)))
                        f(to[n][:, 0:T], part(c, i * N + (base + n), T), ACT.Square).then_inc(sq_ready, 1)
                loop(act, 0, count // N, body)

            def deviation(c, T):
                var = norm_buffers(c)[1]
                act.wait_ge(ln_var, shown(ln_var, LN_NO[c] + 1))
                f(var[:, 0:T], var[:, 0:T], ACT.Sqrt).then_inc(ln_sd, 1)

            def norm_affine(c, T, layer, first=0, last=KT):
                def body(i):
                    act.wait_ge(n_ready, shown(n_ready, At(LN_AT[c] + 1, 1, i)))
                    f(part(c, i, T), part(c, i, T), ACT.Identity, scale=vec(f"ln_g{layer}", i),
                      bias=vec(f"ln_b{layer}", i)).then_inc(x_ready, 1)
                loop(act, first, last, body)

            grant(act, m0_row, acc_free, exp_done, at_evac, vt_evac, t2_evac)
            act.wait_ge(vecs_land, shown(vecs_land, 16))
            f(t1[:, 0:48], vec("c0", 0, 48), ACT.Tanh, scale=0.5).then_inc(setup_act, 1)

            def mod0(i):
                for s in range(2):
                    act.wait_ge(m0_used, shown(m0_used, At(4 * s + 4, 8, i)))
                    act.wait_ge(m0_cols, shown(m0_cols, At(s - 1, 2, i)))
                    f(ev[s][0:2, 0:MC], S[0:2, MC * s:MC * (s + 1)]).then_inc(m0_row, 1)
            mod0(0)
            act.wait_ge(setup_dve, shown(setup_dve, 2))
            f(small[:, 4:8], small[:, 0:4], ACT.Exp).then_inc(setup_act, 1)
            loop(act, 1, MOD0_CHUNKS // 2, mod0)
            hi(At(0))
            act.wait_ge(dve_phase, shown(dve_phase, after("setup")))
            act.wait_ge(late_consts, shown(late_consts, 32))
            act.wait_ge(bias_st, shown(bias_st, 16))
            modulate("c.h", ctx_tile, CTX, *by_set(1))
            for c, layer, l in (("c", 0, 0), ("a", 0, 0), ("b", 2, 1)):
                T = TOK[c]
                which = {"c": 1, "a": 0, "b": 2}[c]
                if c == "a":
                    act.wait_ge(x_land, shown(x_land, 32))
                    act.wait_ge(tile_done, shown(tile_done, TILE0["aconv"]))
                    act.wait_ge(r_done, shown(r_done, 16))
                    modulate("a.h", lambda i: tile(xy, i, SEQ), SEQ, *by_set(0), 0, KT // 2)
                    modulate("a.h", late_x, SEQ, *by_set(0), KT // 2, KT)
                if c == "b":
                    act.wait_ge(tile_done, shown(tile_done, TILE0["bconv"]))
                    act.drain()
                    modulate("b.h", lambda i: tile(xy, i, SEQ), SEQ, *by_set(2))
                conv(c)
                heads(c)
                pooling(c)
                act.wait_ge(dve_phase, shown(dve_phase, after(c + "head")))
                act.wait_ge(tile_done, shown(tile_done, TILE0[c + "out"]))
                if c != "c":
                    split_y(c, T, 0, 12)
                act.wait_ge(dve_phase, shown(dve_phase, after(c + "pool")))
                split_y(c, T, 0 if c == "c" else 12)
                project_out(c, c + "out", which)
                if c == "a":
                    act.wait_ge(x_land, shown(x_land, 48))
                    act.wait_ge(tile_done, shown(tile_done, TILE0["kv1"]))
                    act.wait_ge(r_done, shown(r_done, 32))
                    modulate("kv1", ctx_tile, CTX, *by_set(3))

                    def kv1(i, squares=False):
                        for p in range(2):
                            j, a = j_at("kv1", i, p), a_at("kv1", i, p)
                            hi(j + 1)
                            if squares and p == 0:
                                squares_to_add("a", SEQ, i - 1)
                            if p == 0:
                                act.wait_ge(vt_done, shown(vt_done, At(VT0["kv1"], 1, i)))
                                act.wait_ge(r_done, shown(r_done, 32))
                            else:
                                act.wait_ge(k_st, shown(k_st, At(16 * N_HEADS, 16, i)))
                            act.wait_ge(tile_done, shown(tile_done, j + 1))
                            f((ev[2], kb)[p][:, 0:CTX], acc[a.odd][:, 0:CTX]).then_inc(acc_free, 1)
                        act.wait_ge(vt_done, shown(vt_done, At(VT0["kv1"] + 1, 1, i)))
                        act.wait_ge(v_st, shown(v_st, At(16 * N_HEADS, 16, i)))
                        f(vtok[:, 0:CTX], misc[:, 0:CTX]).then_inc(vt_evac, 1)

                    kv1(0)
                    loop(act, 1, 5, lambda i: kv1(i, squares=True))
                    kv1(5)
                    deviation("a", SEQ)
                    for i in (6, 7):
                        kv1(i)
                        norm_affine("a", SEQ, 0, KT // 2 * (i - 6), KT // 2 * (i - 5))
                if c == "b":
                    squares(c, T, 0, KT)
                    deviation(c, T)
            act.wait_ge(tile_done, shown(tile_done, TILE0["glu"]))
            modulate("g.h", lambda i: tile(xy, i, SEQ), SEQ, lambda k: vec("c0", k), lambda k: vec("c1", k),
                     normed=LN_AT["b"])

            def glu(i, first=False):
                for p in range(6):
                    ch, q = p // 3, p % 3
                    j, a = j_at("glu", i, p), a_at("glu", i, p)
                    hi(j + 1)
                    if first and p < 3:
                        norm_affine("b", SEQ, 1, (0, 6, 11)[p], (6, 11, KT)[p])
                    if q < 2:
                        act.wait_ge(conv_done, shown(conv_done, At(CONV0["glu"] + ch, 2, i)))
                    else:
                        act.wait_ge(gs_done, shown(gs_done, At(ch, 2, i)))
                    act.wait_ge(tile_done, shown(tile_done, j + 1))
                    x = acc[a.odd][:, :]
                    if q == 0:
                        f(ev[0][:], x, scale=0.5).then_inc(acc_free, 1)
                    elif q == 1:
                        f(evt[:], x, ACT.Tanh, scale=0.5).then_inc(acc_free, 1)
                    else:
                        half_and_tanh(x, ev[2][:], ev[3][:]).then_inc(acc_free, 1)
            glu(0, first=True)
            loop(act, 1, 4, glu)
            for p in range(4):
                j, a = j_at("kv2", 0, p), a_at("kv2", 0, p)
                hi(j + 1)
                if p == 2:
                    act.wait_ge(gs_done, shown(gs_done, 8))
                act.wait_ge(tile_done, shown(tile_done, j + 1))
                f((k2[:, 0:512], k2[:, 512:1024], ev[3][:], ev[1][:])[p], acc[a.odd][:, :]).then_inc(acc_free, 1)
            for v in range(2):
                act.wait_ge(vt_done, shown(vt_done, VT0["kv2"] + v + 1))
                f(vtok[:, :].rearrange("p (b n) -> p b n", b=4)[:, :, P * v:P * (v + 1)],
                  misc[:, :].rearrange("p (b n) -> p b n", b=4)).then_inc(vt_evac, 1)
            act.wait_ge(conv_done, shown(conv_done, CONV0["glu"] + 8))
            squares("cln", SEQ, 8, 8)

            def conv_silu(i):
                us = [tile(xy, i * 2 + (6 + s), SEQ) for s in range(2)]
                for s in range(2):
                    act.wait_ge(n_ready, shown(n_ready, At(LN_AT["cln"] + s - 1, 2, i)))
                    act.wait_ge(u2_ready, shown(u2_ready, At(s - 3, 2, i)))
                    f(us[s], us[s], ACT.Identity, scale=vec("cln_g", i * 2 + (s - 2)), bias=vec("cln_b", i * 2 + (s - 2)))
                act.drain()
                for s in range(2):
                    f(ev[2 * s][:], us[s], ACT.Tanh).then_inc(th_done, 1)

            def attn2(i, proj=True, attn=True, silu=False):
                for p in range(2):
                    j, a = j_at("attn2", i, p), a_at("attn2", i, p)
                    if proj:
                        hi(j + 1)
                    if attn and p == 0:
                        for e in range(2):
                            act.wait_ge(m2_ready, shown(m2_ready, At(e - 1, 2, i)))
                            o = 8 + 12 * e
                            for b in range(4):
                                s = s2[e][:, 256 * b + (P if b == 0 else 0):256 * (b + 1)]
                                f(s, s, ACT.Exp, bias=small[:, o + b:o + b + 1],
                                  accum_out=small[:, o + 4 + b:o + 5 + b])
                            f(small[:, o + 8:o + 12], small[:, o:o + 4], ACT.Exp,
                              bias=sink[:, bass.ds(i * 2 + (e - 2), 1)]).then_inc(e2_done, 1)
                    if attn and p == 1:
                        for e in range(2):
                            act.wait_ge(t2_done, shown(t2_done, At(e - 1, 2, i)))
                            f(s2[e][:, P:1024], S[:, 1024 * e + P:1024 * (e + 1)]).then_inc(t2_evac, 1)
                    if silu and p == 1:
                        conv_silu(i)
                    if proj:
                        if p == 1:
                            act.wait_ge(gate_used, shown(gate_used, At(24, 1, i)))
                        act.wait_ge(tile_done, shown(tile_done, j + 1))
                        if p == 0:
                            f(qb[:], acc[a.odd][:, :], scale=QK ** -0.5).then_inc(acc_free, 1)
                            if not attn:
                                deviation("cln", SEQ)
                        else:
                            half_and_tanh(acc[a.odd][:, :], ev[3][:], evt[:]).then_inc(acc_free, 1)
            attn2(0, attn=False)
            loop(act, 1, 5, lambda i: attn2(i, silu=True))
            loop(act, 5, 8, attn2)
            attn2(8, proj=False)

            act.wait_ge(tile_done, shown(tile_done, TILE0["pw"]))
            split_y("g", SEQ, 0, 8, base=8)

            def pw(i):
                for t in range(2):
                    j = j_at("pw", i, t)
                    hi(j + 1)
                    for s in range(2):
                        m = 2 * t + s
                        a = a_at("pw", i, m)
                        act.wait_ge(dve_phase, shown(dve_phase, after("attn2")))
                        act.wait_ge(ypw_done, shown(ypw_done, At(m - 1, 4, i)))
                        if s == 0:
                            act.wait_ge(pw_done, shown(pw_done, At(t + 1, 2, i)))
                        else:
                            act.wait_ge(tile_done, shown(tile_done, j + 1))
                        f(ev[s][:], acc[a.odd][:, :], ACT.Identity,
                          bias=vec("b_pw", i * 4 + m)).then_inc(acc_free, 1)
            loop(act, 0, 2, pw)
            act.wait_ge(dve_phase, shown(dve_phase, after("pw")))
            act.wait_ge(tile_done, shown(tile_done, TILE0["out2"]))
            split_y("g", SEQ)
            project_out("g", "out2", 4)
            squares("g", SEQ, 0, KT)
            deviation("g", SEQ)
            norm_affine("g", SEQ, 2)

        @block.tensor
        def _(pe):
            mm = nc.tensor.matmul

            def product(o, j, ks, w_k0=0, split_before=None, beside=None):
                for n, k in enumerate(ks):
                    if beside is not None and n == 3:
                        beside()
                    if split_before is not None:
                        pe.wait_ge(hlo_done, shown(hlo_done, split_before + k + 1))
                    w = slice(j.odd * D + (w_k0 + n) * P, j.odd * D + (w_k0 + n + 1) * P)
                    T = o.shape[1]
                    x = slice(k * SEQ, k * SEQ + T)
                    mm(o, w_hi[:, w], h_hi[:, x], start=n == 0, stop=False)
                    mm(o, w_hi[:, w], h_lo[:, x], start=False, stop=False)
                    last = mm(o, w_lo[:, w], h_hi[:, x], start=False, stop=n == len(ks) - 1)
                return last

            def weight_tile(j, a, T, h, first=False, beside=None):
                pe.wait_ge(lo_done, shown(lo_done, j + 1))
                pe.wait_ge(acc_free, shown(acc_free, a - 1))
                product(acc[a.odd][:, 0:T], j, range(KT), split_before=h if first else None,
                        beside=beside).then_inc(tile_done, 1)

            def reduce_mod(phase, i):
                q = chunk_at(phase, i)
                pe.wait_ge(macc_ready, shown(macc_ready, q + 1))
                pe.wait_ge(mod_out, shown(mod_out, q))
                for v in range(len(MOD_OF[phase][0])):
                    for s in range(MOD_COLS):
                        n = MOD_COLS * v + s
                        last = mm(mod_ps[:, n:n + 1], macc[:, MC * v + P * s:MC * v + P * (s + 1)], ones[:, 0:1],
                                  start=True, stop=True)
                last.then_inc(mod_red, 1)

            def conv(c):
                phase = c + "conv"

                def body(g, ctx_norm=None):
                    for p in range(4):
                        weight_tile(j_at(phase, g, p), a_at(phase, g, p), TOK[c], H_AT[c + ".h"], p == 0)
                        if phase in CHUNK0 and p == 3:
                            reduce_mod(phase, g)
                        if ctx_norm == 1 and p == 0:
                            added_squares_sum("c", CTX)
                if c == "a":
                    body(0, ctx_norm=0)
                    body(1, ctx_norm=1)
                    loop(pe, 2, N_CONV, body)
                else:
                    loop(pe, 0, N_CONV, body)

            def heads(c):
                T, phase, h0 = TOK[c], c + "head", 8 * PASS[c]
                QT = T // P
                LT = T // P
                ctx_keys = CTX if c != "c" else 0
                NK = T + ctx_keys

                def scores(i, qt):
                    n = At(N0[c] - QT + qt, QT, i)
                    if qt == 0:
                        pe.wait_ge(qk_ready, shown(qk_ready, At(h0, 1, i)))
                        if ctx_keys:
                            pe.wait_ge(k_ld, shown(k_ld, At(16 * (h0 - 8), 16, i)))
                    pe.wait_ge(exp_done, shown(exp_done, n))
                    for m in (1, 0):
                        if m == 0:
                            pe.wait_ge(at_evac, shown(at_evac, n))
                        h = slice(QK * m, QK * (m + 1))
                        q = qb[h, P * qt:P * (qt + 1)]
                        last = mm(S[:, 1024 * m:1024 * m + T], q, kb[h, 0:T], start=True, stop=True)
                        if ctx_keys:
                            last = mm(S[:, 1024 * m + T:1024 * m + NK], q, kb[h, T:NK], start=True, stop=True)
                    last.then_inc(s_ready, 1)

                def transposes(i, qt):
                    pe.wait_ge(a_ready, shown(a_ready, At(N0[c] - QT + qt + 1, QT, i)))
                    for k in range(NK // P):
                        last = nc.tensor.transpose(S[:, P * k:P * (k + 1)], maps[0][:, P * k:P * (k + 1)], ident[:])
                    last.then_inc(t_done, 1)

                def step(i, proj=True, attn=True, norm=True, chunk=0, half=0):
                    for p in range(4):
                        if proj:
                            weight_tile(j_at(phase, i, p), a_at(phase, i, p), T, H_AT[c + ".h"])
                            if phase in CHUNK0 and half and p == 3:
                                if norm:
                                    pe.wait_ge(var_ready, shown(var_ready, At(h0 - 1, 1, i)))
                                pe.wait_ge(vt_evac, shown(vt_evac, At(VT0[c], 1, i)))
                                reduce_mod(phase, chunk)
                        else:
                            weight_tile(j_at(c + "pool", 0, p), a_at(c + "pool", 0, p), T, H_AT[c + ".h"])
                        if attn and p < QT:
                            transposes(i, p)
                            if p + 1 < QT:
                                scores(i, p + 1)
                    if attn:
                        pe.wait_ge(at_evac, shown(at_evac, At(N0[c], QT, i)))
                        pe.wait_ge(vt_evac, shown(vt_evac, At(VT0[c], 1, i)))
                        pe.wait_ge(y_done, shown(y_done, At(h0 - 1, 1, i)))
                        if ctx_keys:
                            pe.wait_ge(v_ld, shown(v_ld, At(16 * (h0 - 8), 16, i)))
                        for k in range(NK // P):
                            last = mm(pv[:, 0:T], vtok[:, P * k:P * (k + 1)], a_t[:, k * T:(k + 1) * T],
                                      start=k == 0, stop=k == NK // P - 1)
                        last.then_inc(pv_done, 1)
                    if proj:
                        pe.wait_ge(acc_free, shown(acc_free, a_at(phase, i, 2) + 1))
                        if norm:
                            pe.wait_ge(var_ready, shown(var_ready, At(h0 - 1, 1, i)))
                        pe.wait_ge(vt_evac, shown(vt_evac, At(VT0[c], 1, i)))
                        if phase in CHUNK0:
                            pe.wait_ge(mod_out, shown(mod_out, chunk_at(phase, chunk, half)))
                        for t in range(LT):
                            last = nc.tensor.transpose(misc[:, P * t:P * (t + 1)], ev[2][:, P * t:P * (t + 1)], ident[:])
                        last.then_inc(vt_done, 1)
                        scores(i + 1, 0)
                    if attn:
                        pe.wait_ge(osq_done, shown(osq_done, At(h0, 1, i)))
                        if proj:
                            pe.wait_ge(vt_evac, shown(vt_evac, At(VT0[c] + 1, 1, i)))
                        else:
                            pe.wait_ge(var_ready, shown(var_ready, At(h0 - 1, 1, i)))
                        mm(misc[:, 0:T], ones[:], osq[:, 0:T], start=True, stop=True).then_inc(ms_done, 1)
                def two_steps(i):
                    step(i * 2, chunk=i)
                    step(i * 2 + 1, chunk=i, half=1)
                step(0, attn=False, norm=False)
                step(1, norm=False, half=1)
                loop(pe, 1, N_HEADS // 2, two_steps)
                step(N_HEADS, proj=False)

            def mix(c, g):
                T = TOK[c]
                pe.wait_ge(box_ready, shown(box_ready, 4 * PASS[c] + g + 1))
                pe.wait_ge(pool_done, shown(pool_done, 4 * PASS[c] + g))
                mm(pv[:, 0:T], work[:, POOLW + P * g:POOLW + P * (g + 1)], work[:, 1584:1584 + T],
                   start=True, stop=True).then_inc(box_mm, 1)

            def pooling(c):
                T, phase = TOK[c], c + "pool"
                for t in range(4, 8):
                    weight_tile(j_at(phase, 0, t), a_at(phase, 0, t), T, H_AT[c + ".h"],
                                beside=(lambda: mix(c, t - 5)) if t >= 6 and T == SEQ else None)
                    if t >= 6 and T < SEQ:
                        mix(c, t - 5)
                    if t == 4:
                        pe.wait_ge(pool_w_land, shown(pool_w_land, 16 * (PASS[c] + 1)))
                        pe.wait_ge(y_done, shown(y_done, 8 * (PASS[c] + 1)))
                        mix(c, 0)
                if T < SEQ:
                    mix(c, 3)

            def project_out(c, phase):
                T = TOK.get(c, SEQ)

                def body(i, beside=None):
                    for p in range(4):
                        weight_tile(j_at(phase, i, p), a_at(phase, i, p), T, H_AT[c + ".y"], p == 0,
                                    beside=beside if p == 0 else None)
                        if phase in CHUNK0 and p == 3:
                            reduce_mod(phase, i)
                if c in "ab":
                    body(0, beside=lambda: mix(c, 3))
                    loop(pe, 1, 4, body)
                else:
                    loop(pe, 0, 4, body)

            def mean(c, T):
                pe.wait_ge(rsum_ready, shown(rsum_ready, LN_NO[c] + 1))
                mm(pv[:, 0:T], ones[:], t1[:, 0:T], start=True, stop=True).then_inc(mean_done, 1)

            def square_sums(c, T, count):
                squares = norm_buffers(c)[3]
                for k in range(count):
                    pe.wait_ge(sq_ready, shown(sq_ready, LN_AT[c] + k + 1))
                    mm(misc[:, 0:T], ones[:], squares[k % len(squares)][:, 0:T], start=k == 0, stop=k == count - 1)\
                        .then_inc(sq_used, 1)

            def added_squares_sum(c, T):
                pe.wait_ge(sqsum_ready, shown(sqsum_ready, LN_NO[c] + 1))
                mm(pv[:, 0:T], ones[:], norm_buffers(c)[1][:, 0:T], start=True, stop=True).then_inc(sq_used, 1)

            grant(pe, m0_used, m0_cols, tile_done, s_ready, t_done, pv_done, vt_done, sq_used, pv2_done)
            pe.wait_ge(setup_dve, shown(setup_dve, 1))

            def mod0_chunk(i, s):
                pe.wait_ge(m0_row, shown(m0_row, At(s - 1, 2, i)))
                for slot in range(4):
                    pe.wait_ge(m0_landed[slot], shown(m0_landed[slot], At(s, 2, i).times(16) + 16))
                    for n in range(D // MC):
                        k = slot * (D // MC) + n
                        last = mm(S[0:2, MC * s:MC * (s + 1)], csil[:, k:k + 17:16],
                                  xy[:, slot * D + n * MC:slot * D + (n + 1) * MC], start=k == 0, stop=k == KT - 1)
                    last.then_inc(m0_used, 1)

            def mod0_columns(i, s):
                pe.wait_ge(m0_row, shown(m0_row, At(s + 1, 2, i)))
                for h in range(MOD_COLS):
                    at = 2 * MOD_COLS * s + 2 * h
                    last = mm(pv[:, bass.ds(i * (4 * MOD_COLS) + at, 2)], ev[s][0:2, P * h:P * (h + 1)], ident[0:2, 0:2],
                              start=True, stop=True)
                last.then_inc(m0_cols, 1)

            def mod0(i, first=False):
                mod0_chunk(i, 0)
                if first:
                    pe.wait_ge(consts, shown(consts, 6 * 16))
                    mm(acc[0][0:16, 0:384], ev[3][0:32, 0:16], ev[3][0:32, 16:400], start=True, stop=True)\
                        .then_inc(setup_pe, 1)
                else:
                    mod0_columns(i - 1, 1)
                mod0_chunk(i, 1)
                mod0_columns(i, 0)
                reduce_mod("mod0", i)
            mod0(0, first=True)
            loop(pe, 1, MOD0_CHUNKS // 2, mod0)
            mod0_columns(MOD0_CHUNKS // 2 - 1, 1)
            for c in "cab":
                conv(c)
                heads(c)
                pooling(c)
                project_out(c, c + "out")
                mean(c, TOK[c])
                if c == "a":
                    def kv1(i):
                        for p in range(2):
                            weight_tile(j_at("kv1", i, p), a_at("kv1", i, p), CTX, H_AT["kv1"], p == 0)
                        pe.wait_ge(acc_free, shown(acc_free, a_at("kv1", i, 0) + 1))
                        pe.wait_ge(vt_evac, shown(vt_evac, At(VT0["kv1"], 1, i)))
                        for t in range(CTX // P):
                            last = nc.tensor.transpose(misc[:, P * t:P * (t + 1)], ev[2][:, P * t:P * (t + 1)], ident[:])
                        last.then_inc(vt_done, 1)
                    loop(pe, 0, 5, kv1)
                    added_squares_sum("a", SEQ)
                    loop(pe, 5, N_HEADS, kv1)
                if c == "b":
                    square_sums(c, TOK[c], KT)
            h2 = H_AT["g.h"]

            def glu(i):
                for p in range(6):
                    weight_tile(j_at("glu", i, p), a_at("glu", i, p), SEQ, h2, p == 0)
            loop(pe, 0, 4, glu)
            for p in range(4):
                weight_tile(j_at("kv2", 0, p), a_at("kv2", 0, p), SEQ, h2)
                if p == 2:
                    mean("cln", SEQ)
            for v in range(2):
                pe.wait_ge(acc_free, shown(acc_free, a_at("kv2", 0, 2 + v) + 1))
                pe.wait_ge(vt_evac, shown(vt_evac, VT0["kv2"] + v))
                for b in range(4):
                    last = nc.tensor.transpose(misc[:, P * b:P * (b + 1)], ev[3 - 2 * v][:, P * b:P * (b + 1)], ident[:])
                last.then_inc(vt_done, 1)
            pe.wait_ge(vt_evac, shown(vt_evac, VT0["kv2"] + 2))
            square_sums("cln", SEQ, 8)

            def attn2(pair, proj=True, attn=True):
                def step(i):
                    if attn:
                        pe.wait_ge(acc_free, shown(acc_free, a_at("attn2", i, -2) + 1))
                        for e in range(2):
                            pe.wait_ge(t2_evac, shown(t2_evac, At(e - 3, 2, i)))
                            h = slice(QK * e, QK * (e + 1))
                            for b in range(4):
                                k0 = 512 * pair + P * max(b - 1, 0)
                                n = 256 if b else P
                                last = mm(S[:, 1024 * e + 256 * (b + 1) - n:1024 * e + 256 * (b + 1)],
                                          qb[h, P * b:P * (b + 1)], k2[h, k0:k0 + n], start=True, stop=True)
                            last.then_inc(s2_ready, 1)
                    if proj:
                        weight_tile(j_at("attn2", i, 0), a_at("attn2", i, 0), SEQ, h2)
                    if attn:
                        for e in range(2):
                            pe.wait_ge(p2_ready, shown(p2_ready, At(e - 1, 2, i)))
                            for t in range(1, 8):
                                last = nc.tensor.transpose(S[:, 1024 * e + P * t:1024 * e + P * (t + 1)],
                                                           s2[e][:, P * t:P * (t + 1)], ident[:])
                            last.then_inc(t2_done, 1)
                    if proj:
                        weight_tile(j_at("attn2", i, 1), a_at("attn2", i, 1), SEQ, h2)
                    if attn:
                        pe.wait_ge(t2_evac, shown(t2_evac, At(0, 2, i)))
                        pe.wait_ge(y2_done, shown(y2_done, At(-1, 1, i)))
                        for e in range(2):
                            for b in range(4):
                                for x in range(2 if b else 1):
                                    v = 256 * (b - x) + QK * (2 * pair + e)
                                    p = 256 * b + (P if x == 0 else 0)
                                    last = mm(pv[QK * e:QK * (e + 1), P * b:P * (b + 1)], vtok[:, v:v + QK],
                                              s2[e][:, p:p + P], start=x == 0, stop=x == (1 if b else 0))
                        last.then_inc(pv2_done, 1)
                return step
            attn2(0, attn=False)(0)
            loop(pe, 1, 5, attn2(0))
            loop(pe, 5, 8, attn2(1))
            attn2(1, proj=False)(8)

            def pw(i):
                for t in range(2):
                    j = j_at("pw", i, t)
                    pe.wait_ge(lo_done, shown(lo_done, j + 1))
                    for s in range(2):
                        a = a_at("pw", i, 2 * t + s)
                        pe.wait_ge(acc_free, shown(acc_free, a - 1))
                        product(acc[a.odd][:, :], j, range(8), 8 * s, H_AT["pw"]).then_inc((pw_done, tile_done)[s], 1)
            loop(pe, 0, 2, pw)
            project_out("g", "out2")
            mean("g", SEQ)
            square_sums("g", SEQ, KT)

        @block.vector
        def _(dve):
            tt, ts, stt = nc.vector.tensor_tensor, nc.vector.tensor_scalar, nc.vector.scalar_tensor_tensor
            phases_done = [0]

            def phase_done(name):
                dve.drain()
                dve.sem_inc(dve_phase, 1)
                assert DVE_PHASES[phases_done[0]] == name, name
                phases_done[0] += 1

            def lo(j):
                dve.wait_ge(hi_done, shown(hi_done, j + 1))
                s = slice(j.odd * D, (j.odd + 1) * D)
                tt(w_lo[:, s], raw[:, s], w_hi[:, s].bitcast(F32), ALU.subtract).then_inc(lo_done, 1)

            def modulated(c, T, i):
                for s in range(2):
                    dve.wait_ge(hhi_done, shown(hhi_done, At(H_AT[c] + s + 1, 2, i)))
                    tt(tile(h_lo, i * 2 + s, T), whole[s][:, 0:T], tile(h_hi, i * 2 + s, T).bitcast(F32),
                       ALU.subtract).then_inc(hlo_done, 1)

            def modulate(c, src, T, scale, bias, first=0, last=KT):
                def body(i):
                    dve.drain()
                    k = i * 2 + 1
                    ts(whole[1][:, 0:T], src(k), scale(k), bias(k), ALU.mult, ALU.add)
                    dve.drain()
                    modulated(c, T, i)
                loop(dve, first // 2, last // 2, body)

            def split_y(c, T, first=0, last=KT, base=0):
                def body(i):
                    for s in range(4):
                        k = i * 4 + s
                        dve.wait_ge(hhi_done, shown(hhi_done, At(H_AT[c] + s + 1, 4, i)))
                        tt(tile(h_lo, k, T), part(c[0], i * 4 + (base + s), T), tile(h_hi, k, T).bitcast(F32),
                           ALU.subtract).then_inc(hlo_done, 1)
                loop(dve, first // 4, last // 4, body)

            def mod_tiles(phase, i, tiles):
                sets, _ = MOD_OF[phase]
                for t in tiles:
                    m = chunk_at(phase, i).times(MOD_TILES) + t
                    for kk in range(MOD_KT):
                        k = MOD_KT * t + kk
                        if k:
                            dve.drain()
                        if kk == 0 and phase == "mod0":
                            dve.wait_ge(gate0_landed[t % 4], shown(gate0_landed[t % 4], At(t // 4, 2, i).times(16) + 16))
                        elif kk == 0:
                            landed = (m - 4 * MOD_TILES).half.times(16) + 16
                            dve.wait_ge(mraw_landed[m.odd], shown(mraw_landed[m.odd], landed))
                        for v, w in enumerate(sets):
                            s = macc[:, MC * v:MC * (v + 1)]
                            slot = gate0[t % 4] if phase == "mod0" else gate0[m.odd]
                            x = slot[:, MC * kk:MC * (kk + 1)]
                            cc = csil[:, 16 * MOD_VEC[w] + k:16 * MOD_VEC[w] + k + 1]
                            last = ts(s, x, cc, None, ALU.mult) if k == 0 else stt(s, x, cc, s, ALU.mult, ALU.add)
                    last.then_inc(mod_used, 1)
                if tiles and tiles[-1] == MOD_TILES - 1:
                    dve.drain()
                    dve.sem_inc(macc_ready, 1)

            def mod_columns(phase, i):
                sets, col = MOD_OF[phase]
                dve.wait_ge(mod_red, shown(mod_red, chunk_at(phase, i) + 1))
                for v, w in enumerate(sets):
                    m = i * MOD_COLS + col
                    last = tt(modc[:, bass.ds(m + 48 * w, MOD_COLS)], mod_ps[:, MOD_COLS * v:MOD_COLS * (v + 1)],
                              vec(f"b_mod{MOD_LAYER[w]}", m, MOD_COLS), ALU.add)
                last.then_inc(mod_out, 1)

            def one_plus(sets):
                dve.drain()
                for w in sets:
                    s = modc[:, 48 * w + 16:48 * w + 32]
                    ts(s, s, 1.0, None, ALU.add)
                dve.drain()

            def conv(c, l):
                T, phase = TOK[c], c + "conv"
                v = work[:, 0:T + 2]
                y, g = t1[:, 0:T], t2[:, 0:T]
                nc.vector.memset(work[:, 0:1], 0.0)
                nc.vector.memset(work[:, T + 1:T + 2], 0.0)
                dve.drain()

                def body(i, ctx_norm=None):
                    for p in range(4):
                        j, a = j_at(phase, i, p), a_at(phase, i, p)
                        lo(j + 1)
                        if ctx_norm == 0:
                            centre("c", CTX, p)
                            if p:
                                add_squares("c", CTX, p - 1)
                        if ctx_norm == 1 and p == 0:
                            add_squares("c", CTX, 3)
                            dve.drain()
                            dve.sem_inc(sqsum_ready, 1)
                        if ctx_norm == 1 and p == 1:
                            variance("c", CTX, KT)
                        if ctx_norm == 1 and p == 3:
                            normalise("c", CTX, 0, KT)
                        if phase in CHUNK0:
                            mod_tiles(phase, i, ((0, 1, 2), (3, 4, 5), (6, 7), ())[p])
                        if p == 2:
                            dve.wait_ge(acc_free, shown(acc_free, a_at(phase, i, 1) + 1))
                            tt(work[:, 1:T + 1], ev[0][:, 0:T], ev[1][:, 0:T], ALU.mult)
                            dve.drain()
                            ts(y, v[:, 0:T], vec(f"conv_w{l}", i), None, ALU.mult)
                            for tap in (1, 2):
                                dve.drain()
                                stt(y, v[:, tap:tap + T], vec(f"conv_w{l}", i + 4 * tap), y, ALU.mult, ALU.add)
                    dve.drain()
                    dve.wait_ge(acc_free, shown(acc_free, a_at(phase, i, 3) + 1))
                    tt(y, y, ev[2][:, 0:T], ALU.mult)
                    stt(g, evt[:, 0:T], 1.0, ev[3][:, 0:T], ALU.add, ALU.mult)
                    dve.drain()
                    tt(part(c, i, T), y, g, ALU.mult).then_inc(conv_done, 1)
                    if phase in CHUNK0:
                        mod_columns(phase, i)
                if c == "a":
                    body(0, ctx_norm=0)
                    body(1, ctx_norm=1)
                    loop(dve, 2, N_CONV, body)
                else:
                    loop(dve, 0, N_CONV, body)
                phase_done(phase)

            def heads(c, l):
                T, phase, h0 = TOK[c], c + "head", 8 * PASS[c]
                QT = T // P
                NK = T + (CTX if c != "c" else 0)
                if c == "a":
                    dve.wait_ge(rope_land, shown(rope_land, 16))
                S3 = S[:, :].rearrange("p (m k) -> p m k", m=2)

                def head_norm(i):
                    dve.wait_ge(sd_done, shown(sd_done, At(h0 - 1, 1, i)))
                    nc.vector.reciprocal(t2[:, 0:T], t2[:, 0:T])
                    dve.drain()
                    tt(t2[:, 0:T], pv[:, 0:T], t2[:, 0:T], ALU.mult)
                    dve.drain()
                    y = part(c, i + 2, T)
                    stt(y, t2[:, 0:T], vec(f"subln{l}"), y, ALU.mult, ALU.mult).then_inc(y_done, 1)

                def mean_square(i):
                    dve.wait_ge(ms_done, shown(ms_done, At(h0 - 1, 1, i)))
                    ts(t2[:, 0:T], misc[:, 0:T], 1.0 / P, EPS, ALU.mult, ALU.add).then_inc(var_ready, 1)

                def step(i, proj=True, attn=True, norm=True, chunk=0, half=0):
                    for p in range(4):
                        n = At(N0[c] - QT + p, QT, i)
                        if attn and p < QT:
                            dve.wait_ge(s_ready, shown(s_ready, n + 1))
                            nc.vector.tensor_reduce(small[:, 0:2], S3[:, :, 0:NK], AX_X, ALU.max,
                                                    negate=True).then_inc(nb_ready, 1)
                        if norm and p == 0:
                            mean_square(i)
                        lo(j_at(phase, i, p) + 1 if proj else j_at(c + "pool", 0, p + 1))
                        if attn and p < QT:
                            dve.wait_ge(exp_done, shown(exp_done, n + 1))
                            nc.vector.reciprocal(small[:, 4:6], small[:, 2:4])
                            dve.drain()
                            ts(small[:, 6:7], small[:, 5:6], lam[:, l:l + 1], None, ALU.mult)
                            dve.drain()
                            ts(maps[1][:, 0:NK], maps[1][:, 0:NK], small[:, 6:7], None, ALU.mult)
                            dve.drain()
                            stt(maps[0][:, 0:NK], maps[0][:, 0:NK], small[:, 4:5], maps[1][:, 0:NK],
                                ALU.mult, ALU.add).then_inc(a_ready, 1)
                        if norm and p == 0:
                            head_norm(i)
                        if proj and phase in CHUNK0 and p in (1, 2):
                            mod_tiles(phase, chunk, (4 * half + 2 * p - 2, 4 * half + 2 * p - 1))
                        if proj and p == 3:
                            dve.drain()
                            dve.wait_ge(acc_free, shown(acc_free, a_at(phase, i, 1) + 1))
                            if attn:
                                dve.wait_ge(s_ready, shown(s_ready, At(N0[c], QT, i)))
                            if c == "c":
                                if attn:
                                    dve.wait_ge(k_st, shown(k_st, At(0, 16, i)))
                                nc.vector.tensor_copy(qb[:, 0:T], ev[0][:, 0:T])
                                nc.vector.tensor_copy(kb[:, 0:T], ev[1][:, 0:T]).then_inc(qk_ready, 1)
                            else:
                                for x, o in ((ev[0], qb), (ev[1], kb)):
                                    if x is ev[1]:
                                        dve.drain()
                                    tt(t2[:], x[:], rope[:, 0:SEQ], ALU.mult)
                                    nc.vector.stream_shuffle(t1[:], x[:], SWAP)
                                    dve.drain()
                                    tt(t1[:], t1[:], rope[:, SEQ:2 * SEQ], ALU.mult)
                                    dve.drain()
                                    last = tt(o[:, 0:SEQ], t1[:], t2[:], ALU.add)
                                last.then_inc(qk_ready, 1)
                    if proj and half and phase in CHUNK0:
                        mod_columns(phase, chunk)
                    if proj:
                        dve.wait_ge(acc_free, shown(acc_free, a_at(phase, i, 3) + 1))
                        if c == "a" and not norm and attn:
                            dve.wait_ge(x_st, shown(x_st, 16))
                        stt(part(c, i + 4, T), evt[:, 0:T], 1.0, ev[3][:, 0:T], ALU.add, ALU.mult).then_inc(gate_used, 1)
                def two_steps(i):
                    step(i * 2, chunk=i)
                    step(i * 2 + 1, chunk=i, half=1)
                step(0, attn=False, norm=False)
                step(1, norm=False, half=1)
                loop(dve, 1, N_HEADS // 2, two_steps)
                step(N_HEADS, proj=False)
                mean_square(N_HEADS + 1)
                head_norm(N_HEADS + 1)
                if phase == "ahead":
                    one_plus((2, 3))
                if phase == "bhead":
                    one_plus((4,))
                    up, shift = modc[:, 48 * 4 + 16:48 * 4 + 32], modc[:, 48 * 4:48 * 4 + 16]
                    tt(vec("c0", 0, KT), vec("ln_g1", 0, KT), up, ALU.mult)
                    tt(vec("c1", 0, KT), vec("ln_b1", 0, KT), up, ALU.mult)
                    dve.drain()
                    tt(vec("c1", 0, KT), vec("c1", 0, KT), shift, ALU.add)
                phase_done(phase)

            def pooling(c, l):
                T, phase = TOK[c], c + "pool"
                L = T + 2 * PAD
                box = [work[:, 528 * n:528 * n + L] for n in range(3)]
                d = work[:, 1584:1584 + T]
                nc.vector.memset(box[0][:, 0:PAD], 0.0)
                nc.vector.memset(box[0][:, PAD + T:L], 0.0)
                for g, w in enumerate(WINDOWS):
                    if T < SEQ:
                        for t in ((5,), (6, 7), (8,), ())[g]:
                            lo(j_at(phase, 0, t))
                    u_in, half, th = ((ev[0], ev[3], evt), (ev[1], ev[2], t1))[g % 2]
                    cut = small[:, 8:24]
                    dve.wait_ge(acc_free, shown(acc_free, a_at(phase, g, 0) + 1))
                    u = box[0][:, PAD:PAD + T]
                    nc.vector.tensor_copy(u, u_in[:, 0:T])
                    src, n, dst = 0, 1, 1
                    while n < w:
                        dve.drain()
                        m = L - 2 * n + 1
                        tt(box[dst][:, 0:m], box[src][:, 0:m], box[src][:, n:n + m], ALU.add)
                        src, n, dst = dst, 2 * n, (2 if dst == 1 else 1)
                    dve.drain()
                    o = PAD - w // 2
                    s = box[src]
                    stt(d, s[:, o:o + T], 1.0 / w, u, ALU.mult, ALU.subtract)
                    for at, e in ((0, 0), (T - 8, 8)):
                        tt(cut[:, e:e + 8], s[:, o + at:o + at + 8], edge[:, 16 * g + e:16 * g + e + 8], ALU.mult)
                    dve.drain()
                    for at, e in ((0, 0), (T - 8, 8)):
                        last = tt(d[:, at:at + 8], cut[:, e:e + 8], u[:, at:at + 8], ALU.subtract)
                    dve.drain()
                    dve.sem_inc(box_ready, 1)
                    if T == SEQ:
                        lo(j_at(phase, 0, g + 5))
                    dve.wait_ge(acc_free, shown(acc_free, a_at(phase, g, 1) + 1))
                    stt(t2[:, 0:T], th[:, 0:T], 1.0, half[:, 0:T], ALU.add, ALU.mult)
                    dve.drain()
                    if g == 3 and T == SEQ:
                        split_y(c + ".y", T, 0, 12)
                    dve.wait_ge(box_mm, shown(box_mm, 4 * PASS[c] + g + 1))
                    stt(part(c, 12 + g, T), pv[:, 0:T], vec(f"pool_s{l}", g), t2[:, 0:T],
                        ALU.mult, ALU.mult).then_inc(pool_done, 1)
                phase_done(phase)

            def project_out(c, phase, alpha):
                T = TOK.get(c, SEQ)
                nc.vector.memset(t1[:, 0:T], 0.0)
                dve.drain()

                def body(i, last=False):
                    for p in range(4):
                        if not (last and p == 3):
                            lo(j_at(phase, i, p) + 1)
                        if phase in CHUNK0:
                            mod_tiles(phase, i, (2 * p, 2 * p + 1))
                        dve.wait_ge(acc_free, shown(acc_free, a_at(phase, i, p) + 1))
                        dve.wait_ge(xin_land[p % 2], shown(xin_land[p % 2], At(R_AT[c] // 2 + p // 2, 2, i).times(16) + 16))
                        r = part(c, i * 4 + p, T)
                        stt(r, (qb, kb)[p % 2][:, 0:T], alpha, ev[p][:, 0:T], ALU.mult, ALU.add)
                        dve.drain()
                        tt(t1[:, 0:T], t1[:, 0:T], r, ALU.add).then_inc(r_done, 1)
                    if phase in CHUNK0:
                        mod_columns(phase, i)
                if phase == "out2":
                    loop(dve, 0, 3, body)
                    body(3, last=True)
                else:
                    loop(dve, 0, 4, body)
                dve.drain()
                dve.sem_inc(rsum_ready, 1)
                phase_done(phase)

            def less_mean(c, T, count):
                mean = norm_buffers(c)[0]
                dve.wait_ge(mean_done, shown(mean_done, LN_NO[c] + 1))
                ts(mean[:, 0:T], pv[:, 0:T], 1.0 / (count * P), None, ALU.mult)
                dve.drain()

            def centred(c, T, base, count):
                less_mean(c, T, count)

                def centre(i):
                    for n in range(4):
                        x = tile(xy, i * 4 + (base + n), T)
                        tt(x, x, t2[:, 0:T], ALU.subtract).then_inc(d_ready, 1)
                loop(dve, 0, count // 4, centre)

            def centre(c, T, g):
                for n in range(4):
                    x = part(c, g * 4 + n, T)
                    tt(x, x, norm_buffers(c)[0][:, 0:T], ALU.subtract).then_inc(d_ready, 1)

            def add_squares(c, T, g):
                _, var, _, squares = norm_buffers(c)
                for n in range(4):
                    dve.drain()
                    dve.wait_ge(sq_ready, shown(sq_ready, At(LN_AT[c] + n + 1, 4, g)))
                    tt(var[:, 0:T], var[:, 0:T], squares[n][:, 0:T], ALU.add).then_inc(sq_added, 1)

            def variance(c, T, count):
                _, var, bank, _ = norm_buffers(c)
                dve.wait_ge(sq_used, shown(sq_used, SQ_AT[c] + (1 if c in "ca" else count)))
                ts(var[:, 0:T], bank[:, 0:T], 1.0 / (count * P), EPS, ALU.mult, ALU.add).then_inc(ln_var, 1)

            def normalise(c, T, base, count, first=True):
                var = norm_buffers(c)[1]
                if first:
                    dve.wait_ge(ln_sd, shown(ln_sd, LN_NO[c] + 1))
                    nc.vector.reciprocal(var[:, 0:T], var[:, 0:T])
                    dve.drain()

                def scale(i):
                    for n in range(min(count, 4)):
                        x = part(c, i * 4 + (base + n), T)
                        tt(x, x, var[:, 0:T], ALU.mult).then_inc(n_ready, 1)
                if count <= 4:
                    scale(0)
                else:
                    loop(dve, 0, count // 4, scale)

            nc.vector.memset(ones[:], 1.0)
            grant(dve, lo_done, hlo_done, sq_added, mod_used, mod_out, conv_done, qk_ready, gate_used, var_ready, y_done, r_done, b_used,
                  u2_ready, ypw_done, pool_done, y2_done, gs_done)
            dve.wait_ge(vecs_land, shown(vecs_land, 16))
            dve.wait_ge(setup_act, shown(setup_act, 1))
            stt(t2[:, 0:48], t1[:, 0:48], 1.0, vec("c0", 0, 48), ALU.add, ALU.mult)
            dve.drain()
            ts(csil[:], t2[:, 0:48], 0.5, None, ALU.mult)
            dve.drain()
            dve.sem_inc(setup_dve, 1)

            def mod0(i):
                mod_tiles("mod0", i, range(MOD_TILES))
                mod_columns("mod0", i)
            mod0(0)
            dve.wait_ge(consts, shown(consts, 6 * 16))
            pairs = ev[2][:, :].rearrange("p (a s d) -> p a s d", s=2, d=QK)
            t1p = t1[:, 0:256].rearrange("p (a d) -> p a d", d=QK)
            tt(t1p, pairs[:, :, 0, :], pairs[:, :, 1, :], ALU.mult)
            dve.drain()
            nc.vector.tensor_reduce(small[:, 0:4], t1p, AX_X, ALU.add).then_inc(setup_dve, 1)
            dve.wait_ge(setup_act, shown(setup_act, 2))
            for l in range(DEPTH):
                tt(lam[:, l:l + 1], small[:, 5 + 2 * l:6 + 2 * l], small[:, 4 + 2 * l:5 + 2 * l], ALU.subtract)
                s = vec(f"subln{l}")
                ts(s, s, 1.0 - LAM_INIT[l], None, ALU.mult)
            dve.drain()
            for l in range(DEPTH):
                ts(lam[:, l:l + 1], lam[:, l:l + 1], -LAM_INIT[l], None, ALU.add)
            for name in ("cln_g", "cln_b"):
                s = vec(name, 0, 8)
                ts(s, s, 0.5, None, ALU.mult)
            dve.wait_ge(setup_pe, shown(setup_pe, 1))
            tt(evt[0:16, 0:384], evt[0:16, 0:384], acc[0][0:16, 0:384], ALU.add).then_inc(setup_dve, 1)
            loop(dve, 1, 4, mod0)
            lo(At(0))
            dve.wait_ge(m0_cols, shown(m0_cols, MOD0_CHUNKS))
            for w in range(2):
                tt(modc[:, 48 * w:48 * w + 32], pv[:, 0:64].rearrange("p (m v) -> p m v", v=2)[:, :, w],
                   vec("b_mod0", 0, 32), ALU.add)
            one_plus((0, 1))
            phase_done("setup")
            dve.wait_ge(late_consts, shown(late_consts, 32))
            modulate("c.h", ctx_tile, CTX, *by_set(1))
            for c, l in (("c", 0), ("a", 0), ("b", 1)):
                T = TOK[c]
                if c == "a":
                    dve.wait_ge(x_land, shown(x_land, 32))
                    modulate("a.h", lambda i: tile(xy, i, SEQ), SEQ, *by_set(0), 0, KT // 2)
                    modulate("a.h", late_x, SEQ, *by_set(0), KT // 2, KT)
                    less_mean("c", CTX, KT)
                    nc.vector.memset(norm_buffers("c")[1], 0.0)
                if c == "b":
                    dve.wait_ge(x_ready, shown(x_ready, 32))
                    modulate("b.h", lambda i: tile(xy, i, SEQ), SEQ, *by_set(2))
                    dve.wait_ge(x_st, shown(x_st, 32))
                conv(c, l)
                heads(c, l)
                pooling(c, l)
                split_y(c + ".y", T, 12 if T == SEQ else 0)
                project_out(c, c + "out", ALPHA1)
                if c == "a":
                    dve.wait_ge(x_land, shown(x_land, 48))
                    modulate("kv1", ctx_tile, CTX, *by_set(3))

                    less_mean("a", SEQ, KT)
                    nc.vector.memset(norm_buffers("a")[1][:], 0.0)

                    def kv1(i):
                        for p in range(2):
                            lo(j_at("kv1", i, p) + 1)

                    def kv1_norm(i):
                        lo(j_at("kv1", i, 0) + 1)
                        centre("a", SEQ, i)
                        add_squares("a", SEQ, i - 1)
                        lo(j_at("kv1", i, 1) + 1)
                    kv1(0)
                    centre("a", SEQ, 0)
                    loop(dve, 1, 4, kv1_norm)
                    lo(j_at("kv1", 4, 0) + 1)
                    add_squares("a", SEQ, 3)
                    dve.drain()
                    dve.sem_inc(sqsum_ready, 1)
                    lo(j_at("kv1", 4, 1) + 1)
                    kv1(5)
                    variance("a", SEQ, KT)
                    kv1(6)
                    normalise("a", SEQ, 0, KT // 2)
                    kv1(7)
                    normalise("a", SEQ, KT // 2, KT // 2, first=False)
                    phase_done("kv1")
                if c == "b":
                    centred(c, T, 0, KT)
                    variance(c, T, KT)
            normalise("b", SEQ, 0, 2)

            def next_pair(i):
                for s in range(2):
                    x = tile(xy, i * 2 + s, SEQ)
                    tt(x, x, t1[:], ALU.mult).then_inc(n_ready, 1)
                modulated("g.h", SEQ, i - 1)
            loop(dve, 1, KT // 2, next_pair)
            modulated("g.h", SEQ, KT // 2 - 1)
            dve.drain()
            nc.vector.memset(work[:, 0:TAPS - 1], 0.0)
            nc.vector.memset(t1[:], 0.0)
            dve.drain()
            TAP_PARTS = (range(0, 11), range(11, 21), range(21, TAPS))

            def taps(c, part):
                u = tile(xy, c + 8, SEQ)
                for tap in TAP_PARTS[part]:
                    if tap == 0:
                        ts(u, work[:, 0:SEQ], vec("dw", c * TAPS), vec("dw_b", c), ALU.mult, ALU.add)
                    else:
                        dve.drain()
                        stt(u, work[:, tap:tap + SEQ], vec("dw", c * TAPS + tap), u, ALU.mult, ALU.add)
                if part == 2:
                    dve.drain()
                    tt(t1[:], t1[:], u, ALU.add)
                    dve.drain()

            def glu(i, first=False):
                for ch in range(2):
                    for q in range(3):
                        lo(j_at("glu", i, 3 * ch + q) + 1)
                        if first and ch and q == 0:
                            dve.wait_ge(x_st, shown(x_st, 48))
                        if ch or not first:
                            taps(i * 2 + (ch - 1), q)
                    dve.wait_ge(acc_free, shown(acc_free, a_at("glu", i, 3 * ch + 1) + 1))
                    stt(work[:, TAPS - 1:TAPS - 1 + SEQ], evt[:], 1.0, ev[0][:], ALU.add, ALU.mult).then_inc(conv_done, 1)
                    dve.drain()
                    dve.wait_ge(acc_free, shown(acc_free, a_at("glu", i, 3 * ch + 2) + 1))
                    stt(gates[:, bass.ds(i * 1024 + 512 * ch, SEQ)], ev[3][:], 1.0, ev[2][:],
                        ALU.add, ALU.mult).then_inc(gs_done, 1)
            glu(0, first=True)
            loop(dve, 1, 4, glu)
            for p in range(4):
                lo(j_at("kv2", 0, p) + 1)
                if p < 3:
                    taps(7, p)
                if p == 2:
                    dve.sem_inc(rsum_ready, 1)
            centred("cln", SEQ, 8, 8)
            dve.wait_ge(vt_evac, shown(vt_evac, VT0["kv2"] + 2))
            phase_done("kv2")
            variance("cln", SEQ, 8)

            def conv_silu(i):
                for s in range(2):
                    dve.wait_ge(th_done, shown(th_done, At(s - 1, 2, i)))
                    u = tile(xy, i * 2 + (6 + s), SEQ)
                    stt(u, ev[2 * s][:], 1.0, u, ALU.add, ALU.mult).then_inc(u2_ready, 1)

            def attn2(i, proj=True, attn=True, silu=False):
                B = ev[1][:, :].rearrange("p (e k) -> p e k", e=2)
                for p in range(2):
                    if proj:
                        lo(j_at("attn2", i, p) + 1)
                    if not attn and p == 1:
                        normalise("cln", SEQ, 8, 8)
                    if attn and p == 0:
                        dve.wait_ge(b_ld, shown(b_ld, At(0, 32, i)))
                        dve.wait_ge(pv2_done, shown(pv2_done, At(-1, 1, i)))
                        for e in range(2):
                            o = 8 + 12 * e
                            dve.wait_ge(s2_ready, shown(s2_ready, At(e - 1, 2, i)))
                            last = tt(s2[e][:, P:256], S[:, 1024 * e + P:1024 * e + 256], B[:, e, P:256], ALU.add)
                            last = tt(s2[e][:, 256:1024].rearrange("p (b k) -> p b k", b=3),
                                      S[:, 1024 * e + 256:1024 * (e + 1)].rearrange("p (b k) -> p b k", b=3),
                                      B[:, e:e + 1, :].broadcast_to([P, 3, 256]), ALU.add)
                            dve.drain()
                            if e == 1:
                                dve.sem_inc(b_used, 1)
                            nc.vector.tensor_reduce(small[:, o:o + 1], s2[e][:, P:256], AX_X, ALU.max)
                            nc.vector.tensor_reduce(small[:, o + 1:o + 4],
                                                    s2[e][:, 256:1024].rearrange("p (b k) -> p b k", b=3), AX_X, ALU.max)
                            dve.drain()
                            ts(small[:, o:o + 4], small[:, o:o + 4], sink[:, bass.ds(i * 2 + (e - 2), 1)], -1.0,
                               ALU.max, ALU.mult).then_inc(m2_ready, 1)
                        for e in range(2):
                            o = 8 + 12 * e
                            dve.wait_ge(e2_done, shown(e2_done, At(e - 1, 2, i)))
                            r = small[:, o + 4:o + 8]
                            tt(r, r, small[:, o + 8:o + 12], ALU.add)
                            dve.drain()
                            nc.vector.reciprocal(r, r)
                            dve.drain()
                            for b in range(4):
                                s = s2[e][:, 256 * b + (P if b == 0 else 0):256 * (b + 1)]
                                last = ts(s, s, small[:, o + 4 + b:o + 5 + b], None, ALU.mult)
                            last.then_inc(p2_ready, 1)
                if proj:
                    dve.wait_ge(acc_free, shown(acc_free, a_at("attn2", i, 1) + 1))
                    stt(tile(xy, i, SEQ), evt[:], 1.0, ev[3][:], ALU.add, ALU.mult).then_inc(gate_used, 1)
                if silu:
                    conv_silu(i)
                if attn:
                    dve.wait_ge(pv2_done, shown(pv2_done, At(0, 1, i)))
                    y = tile(xy, i - 1, SEQ)
                    tt(y, pv[:, :], y, ALU.mult).then_inc(y2_done, 1)
            attn2(0, attn=False)
            loop(dve, 1, 5, lambda i: attn2(i, silu=True))
            loop(dve, 5, 8, attn2)
            attn2(8, proj=False)
            phase_done("attn2")

            split_y("pw", SEQ, 0, 8, base=8)

            def pw(i):
                for t in range(2):
                    lo(j_at("pw", i, t) + 1)
                    for s in range(2):
                        m = 2 * t + s
                        dve.wait_ge(acc_free, shown(acc_free, a_at("pw", i, m) + 1))
                        tt(tile(xy, i * 4 + (8 + m), SEQ), ev[s][:], gates[:, bass.ds(i * 2048 + 512 * m, SEQ)],
                           ALU.mult).then_inc(ypw_done, 1)
            loop(dve, 0, 2, pw)
            phase_done("pw")
            split_y("g.y", SEQ)
            project_out("g", "out2", ALPHA2)
            centred("g", SEQ, 0, KT)
            variance("g", SEQ, KT)
            normalise("g", SEQ, 0, KT)


SWAP = [i ^ 16 for i in range(32)]


def rope_tables():
    n = QK // 4
    inv = np.float32(10000.0) ** (-np.arange(n, dtype=np.float32) / np.float32(n))
    t = np.arange(SEQ)
    rows, cols = (t // 64).astype(np.float32), (t % 64).astype(np.float32)
    f = np.arange(P) % QK
    pos = np.where((f < QK // 2)[:, None], rows[None], cols[None])
    ang = (pos * inv[f % n][:, None]).astype(np.float32)
    sign = np.where(f % (QK // 2) < n, -1.0, 1.0)[:, None]
    return np.concatenate([np.cos(ang), np.sin(ang) * sign], axis=1).astype(np.float32)


def edge_table():
    T = 64
    out = np.zeros((4, 16), np.float32)
    for g, w in enumerate(WINDOWS):
        for e in range(16):
            t = e if e < 8 else T - 16 + e
            lo, hi = max(t - w // 2, 0), min(t + w - w // 2, T)
            out[g, e] = np.float32(1) / np.float32(hi - lo)
    return np.ascontiguousarray(np.broadcast_to(out.reshape(1, 64), (P, 64)))


def distance_tables():
    d = np.arange(P)
    x = np.maximum(d, 1).astype(np.float32)
    large = 16 + (np.log(x / np.float32(16)) / np.float32(math.log(8)) * np.float32(16)).astype(np.int32)
    bucket = np.where(d < 16, d, np.minimum(large, 31))
    onehot = np.zeros((32, 384), np.float32)
    bar = np.full((16, 384), NEG, np.float32)
    for c in range(P, 256):
        onehot[bucket[255 - c], c] = 1.0
        bar[:, c] = 0.0
    return onehot, bar


def kernel(x, c, ctx, c_ctx, w_mod, b_mod, w_in, conv_w, lam_q1, lam_k1, lam_q2, lam_k2, subln_g,
           pool_w, pool_scale, w_out, ln_g, ln_b, c_2, w_ada_2, b_ada_2, w_in_2, rel_bias_2, sinks_2,
           conv_w_2, conv_b_2, conv_ln_g_2, conv_ln_b_2, w_pw_2, b_pw_2, w_out_2, ln_g_2, ln_b_2):
    import concourse.bacc as bacc
    from concourse.bass_utils import run_bass_kernel_spmd

    def cols(a):
        return np.asarray(a).reshape(-1, P).T

    def tiles(w):
        w = np.asarray(w)
        k, n = w.shape
        return w.reshape(k // P, P, n // P, P).transpose(2, 1, 0, 3).reshape(n // P, P, k)

    def tokens(a):
        return np.ascontiguousarray(np.asarray(a)[0].T.reshape(KT, P, -1).transpose(1, 0, 2))

    def by_group(t):
        order = [g + 4 * p for g in range(4) for p in (0, 2, 1, 3)]
        order += [16 + h + 8 * p for h in range(8) for p in range(4)]
        order += [48 + g + 4 * p for g in range(4) for p in range(2)]
        return t[order]

    def mod_weight(w):
        w = np.asarray(w)
        return w.reshape(MOD_TILES, MOD_KT, P, -1, MC).transpose(3, 0, 2, 1, 4).reshape(-1, P, MOD_KT * MC)

    heads2 = [4 * (2 * pair + e) + g for pair in range(2) for g in range(4) for e in range(2)]
    head_cols = np.concatenate([np.arange(64 * h, 64 * h + 64) for h in heads2])
    w2 = np.asarray(w_in_2)[0]
    q2, k2, v2, g2, ga, gb, gc = np.split(w2, np.cumsum([1024, 256, 256, 1024, 1024, 1024]), axis=1)
    q2, g2, ga, gb, gc = (tiles(a) for a in (q2[:, head_cols], g2[:, head_cols], ga, gb, gc))
    weave = lambda *a: np.stack(a, axis=1).reshape(-1, P, D)
    pw = tiles(np.asarray(w_pw_2)[0]).reshape(4, 2, P, D // 2).transpose(0, 2, 1, 3).reshape(4, P, D)
    wo2 = np.asarray(w_out_2)[0]
    wo2 = np.concatenate([wo2[:1024][head_cols], wo2[1024:]], axis=0)

    w_in, w_out = np.asarray(w_in), np.asarray(w_out)
    conv_w, ln_g, ln_b = np.asarray(conv_w), np.asarray(ln_g), np.asarray(ln_b)
    b_mod, pool_scale, subln_g = np.asarray(b_mod), np.asarray(pool_scale), np.asarray(subln_g)
    lams = [np.asarray(a) for a in (lam_q1, lam_k1, lam_q2, lam_k2)]
    vec = {"b_mod0": cols(b_mod[0]), "b_mod1": cols(b_mod[1]), "b_mod2": cols(b_ada_2),
           "conv_w0": cols(conv_w[0]), "conv_w1": cols(conv_w[1]),
           "subln0": cols(subln_g[0]), "subln1": cols(subln_g[1]),
           "pool_s0": cols(pool_scale[0]), "pool_s1": cols(pool_scale[1]),
           "ln_g0": cols(ln_g[0]), "ln_g1": cols(ln_g[1]), "ln_g2": cols(ln_g_2),
           "ln_b0": cols(ln_b[0]), "ln_b1": cols(ln_b[1]), "ln_b2": cols(ln_b_2),
           "dw": np.asarray(conv_w_2)[0].reshape(TAPS, 8, P).transpose(2, 1, 0).reshape(P, 8 * TAPS),
           "dw_b": cols(conv_b_2), "cln_g": cols(conv_ln_g_2), "cln_b": cols(conv_ln_b_2), "b_pw": cols(b_pw_2),
           "c0": cols(c), "c1": cols(c_ctx), "c2": cols(c_2)}
    onehot, bar = distance_tables()
    arrays = {
        "w0": np.concatenate([by_group(tiles(w_in[0])), tiles(w_out[0])]),
        "w1": np.concatenate([by_group(tiles(w_in[1])), tiles(w_out[1])]),
        "w2": np.concatenate([weave(ga, gb, gc), tiles(k2), tiles(v2), weave(q2, g2), pw, tiles(wo2)]),
        "wm": np.concatenate([mod_weight(w_mod[0]), mod_weight(w_mod[1]), mod_weight(np.asarray(w_ada_2)[0])]),
        "xT": tokens(x), "ctxT": tokens(ctx),
        "vecs": np.concatenate([vec[n] for n, _ in VECS], axis=1),
        "lam": np.stack([lams[2 * a + s][l] for l in range(DEPTH) for a in range(2) for s in range(2)]).reshape(512),
        "sinks": np.asarray(sinks_2)[0][heads2],
        "rel_bias": np.asarray(rel_bias_2)[:, heads2],
        "pool_w": np.asarray(pool_w).transpose(0, 2, 1, 3).reshape(DEPTH, P, 512),
        "ident": np.eye(P, dtype=np.float32), "rope": rope_tables(), "edge": edge_table(),
        "onehot": onehot, "negmask": bar,
    }
    arrays = {f"in_{n}": np.ascontiguousarray(a) for n, a in arrays.items()}
    nc = bacc.Bacc("TRN2", target_bir_lowering=False, num_devices=1)
    aps = {n[3:]: nc.dram_tensor(n, a.shape, F32, kind="ExternalInput").ap() for n, a in arrays.items()}
    out = nc.dram_tensor("out_y", (P, KT, SEQ), F32, kind="ExternalOutput").ap()
    build(nc, aps, out)
    r = run_bass_kernel_spmd(nc, [arrays], core_ids=[0])
    y = r.results[0]["out_y"]
    return np.ascontiguousarray(y.transpose(1, 0, 2).reshape(D, SEQ).T)[None]
```
